# Optimizing a Trainium2 kernel written in Bass

```python
import math
import jax
import jax.numpy as jnp
from jax import lax
import numpy as np

D_MODEL = 1024
BATCH = 1
SEQ = 1024
DEPTH = 1

N_MIXERS = 3
N_POOL_LAYERS = len(range(0, DEPTH, N_MIXERS))
N_SC_LAYERS = len(range(1, DEPTH, N_MIXERS))
N_CF_LAYERS = len(range(2, DEPTH, N_MIXERS))

POOL_WINDOWS = (2, 4, 8, 16)
N_POOL_GROUPS = len(POOL_WINDOWS)
POOL_GROUP_DIM = D_MODEL // N_POOL_GROUPS
MAX_POOL = max(POOL_WINDOWS)

SHORT_CONV_WIDTH = 3
CONFORMER_KERNEL = 31

N_EXPERTS = 32
TOP_K = 4
EXPERT_DIM = D_MODEL
SWIGLU_LIMIT = 7.0
SWIGLU_ALPHA = 1.702
EXPERT_BLOCK = 128

DEEPNORM_ALPHA = (2.0 * DEPTH) ** 0.25
DEEPNORM_BETA = (8.0 * DEPTH) ** -0.25
LN_EPS = 1e-5

kernel_name = "hybrid_pool_shortconv_conformer_moe_deepnorm"

def layer_norm(x, g, b):
    xf = x.astype(jnp.float32)
    mu = jnp.mean(xf, axis=-1, keepdims=True)
    xc = xf - mu
    var = jnp.mean(xc * xc, axis=-1, keepdims=True)
    y = xc * lax.rsqrt(var + LN_EPS) * g.astype(jnp.float32) + b.astype(jnp.float32)
    return y.astype(x.dtype)

def causal_depthwise_conv(u, w):
    k = w.shape[0]
    return lax.conv_general_dilated(
        u, w[:, None, :].astype(u.dtype), window_strides=(1,), padding=[(k - 1, 0)],
        dimension_numbers=("NWC", "WIO", "NWC"), feature_group_count=u.shape[-1])

def pool_mixer(x, w_groups, scale):
    seq = x.shape[1]
    xf = x.astype(jnp.float32)
    csum = jnp.pad(jnp.cumsum(xf, axis=1), ((0, 0), (MAX_POOL, 0), (0, 0)))
    outs = []
    for g, win_len in enumerate(POOL_WINDOWS):
        sl = slice(g * POOL_GROUP_DIM, (g + 1) * POOL_GROUP_DIM)
        window_sum = csum[:, MAX_POOL:, sl] - csum[:, MAX_POOL - win_len:MAX_POOL - win_len + seq, sl]
        count = jnp.minimum(jnp.arange(1, seq + 1, dtype=jnp.float32), float(win_len))
        diff = window_sum / count[None, :, None] - xf[..., sl]
        outs.append(jnp.einsum("bsc,ce->bse", diff.astype(x.dtype), w_groups[g]))
    return jnp.concatenate(outs, axis=-1) * scale

def short_conv_mixer(x, w_in, conv_w, w_out):
    proj = jnp.einsum("bsd,de->bse", x, w_in)
    gate_b, gate_c, h = jnp.split(proj, 3, axis=-1)
    u = causal_depthwise_conv(gate_c * h, conv_w)
    return jnp.einsum("bsd,de->bse", gate_b * u, w_out)

def conformer_conv_mixer(x, w_in, b_in, dw_w, dw_b, ln_g, ln_b, w_out, b_out):
    a, gate = jnp.split(jnp.einsum("bsd,de->bse", x, w_in) + b_in, 2, axis=-1)
    u = a * jax.nn.sigmoid(gate)
    u = causal_depthwise_conv(u, dw_w) + dw_b
    u = jax.nn.silu(layer_norm(u, ln_g, ln_b))
    return jnp.einsum("bsd,de->bse", u, w_out) + b_out

def expert_ffn(xb, w_gu, b_gu, w_dn, b_dn):
    h = xb @ w_gu + b_gu
    g = jnp.minimum(h[..., 0::2], SWIGLU_LIMIT)
    up = jnp.clip(h[..., 1::2], -SWIGLU_LIMIT, SWIGLU_LIMIT)
    glu = g * jax.nn.sigmoid(SWIGLU_ALPHA * g)
    return ((up + 1.0) * glu) @ w_dn + b_dn

def moe_ffn(x, router_w, router_b, w_gu, b_gu, w_dn, b_dn):
    bsz, seq, d = x.shape
    n_tok = bsz * seq
    x2d = x.reshape(n_tok, d)
    logits = jnp.dot(x2d.astype(jnp.float32), router_w.astype(jnp.float32)) + router_b.astype(jnp.float32)
    top_vals, top_idx = lax.top_k(logits, TOP_K)
    gates = jax.nn.softmax(top_vals, axis=-1)

    n_assign = n_tok * TOP_K
    flat_e = top_idx.reshape(n_assign).astype(jnp.int32)
    flat_tok = jnp.arange(n_assign, dtype=jnp.int32) // TOP_K
    order = jnp.argsort(flat_e)
    sorted_e = flat_e[order]
    sorted_tok = flat_tok[order]

    counts = jnp.bincount(flat_e, length=N_EXPERTS).astype(jnp.int32)
    padded_counts = ((counts + EXPERT_BLOCK - 1) // EXPERT_BLOCK) * EXPERT_BLOCK
    padded_end = jnp.cumsum(padded_counts)
    padded_start = padded_end - padded_counts
    group_start = jnp.cumsum(counts) - counts
    rank = jnp.arange(n_assign, dtype=jnp.int32) - group_start[sorted_e]
    dest = padded_start[sorted_e] + rank

    n_blocks = -(-n_assign // EXPERT_BLOCK) + N_EXPERTS
    n_pad = n_blocks * EXPERT_BLOCK
    row_tok = jnp.zeros((n_pad,), jnp.int32).at[dest].set(sorted_tok)
    block_start = jnp.arange(n_blocks, dtype=jnp.int32) * EXPERT_BLOCK
    block_expert = jnp.minimum(jnp.searchsorted(padded_end, block_start, side="right"),
                               N_EXPERTS - 1).astype(jnp.int32)

    xs = x2d[row_tok].reshape(n_blocks, EXPERT_BLOCK, d)

    def run_block(args):
        xb, e = args
        return expert_ffn(xb, w_gu[e], b_gu[e], w_dn[e], b_dn[e])

    ys = lax.map(run_block, (xs, block_expert)).reshape(n_pad, d)
    assign_row = jnp.zeros((n_assign,), jnp.int32).at[order].set(dest)
    y = ys[assign_row].reshape(n_tok, TOP_K, d)
    out = jnp.einsum("tk,tkd->td", gates.astype(y.dtype), y)
    return out.reshape(bsz, seq, d)

def setup_inputs(seed: int = 0) -> dict:
    key = jax.random.key(seed)
    keys = iter(jax.random.split(key, 32))

    def nrm(shape, scale):
        return scale * jax.random.normal(next(keys), shape, jnp.float32)

    d, f = D_MODEL, EXPERT_DIM
    return {
        "x": nrm((BATCH, SEQ, d), 1.0),
        "pool_w": nrm((N_POOL_LAYERS, N_POOL_GROUPS, POOL_GROUP_DIM, POOL_GROUP_DIM),
                      DEEPNORM_BETA * POOL_GROUP_DIM ** -0.5),
        "pool_scale": 1.0 + nrm((N_POOL_LAYERS, d), 0.1),
        "sc_w_in": nrm((N_SC_LAYERS, d, 3 * d), d ** -0.5),
        "sc_conv_w": nrm((N_SC_LAYERS, SHORT_CONV_WIDTH, d), SHORT_CONV_WIDTH ** -0.5),
        "sc_w_out": nrm((N_SC_LAYERS, d, d), DEEPNORM_BETA * d ** -0.5),
        "cf_w_in": nrm((N_CF_LAYERS, d, 2 * d), d ** -0.5),
        "cf_b_in": nrm((N_CF_LAYERS, 2 * d), 0.02),
        "cf_dw_w": nrm((N_CF_LAYERS, CONFORMER_KERNEL, d), CONFORMER_KERNEL ** -0.5),
        "cf_dw_b": nrm((N_CF_LAYERS, d), 0.02),
        "cf_ln_g": 1.0 + nrm((N_CF_LAYERS, d), 0.02),
        "cf_ln_b": nrm((N_CF_LAYERS, d), 0.02),
        "cf_w_out": nrm((N_CF_LAYERS, d, d), DEEPNORM_BETA * d ** -0.5),
        "cf_b_out": nrm((N_CF_LAYERS, d), 0.02),
        "mix_ln_g": 1.0 + nrm((DEPTH, d), 0.02),
        "mix_ln_b": nrm((DEPTH, d), 0.02),
        "router_w": nrm((DEPTH, d, N_EXPERTS), d ** -0.5),
        "router_b": nrm((DEPTH, N_EXPERTS), 0.01),
        "moe_w_gu": nrm((DEPTH, N_EXPERTS, d, 2 * f), d ** -0.5),
        "moe_b_gu": nrm((DEPTH, N_EXPERTS, 2 * f), 0.02),
        "moe_w_dn": nrm((DEPTH, N_EXPERTS, f, d), DEEPNORM_BETA * f ** -0.5),
        "moe_b_dn": nrm((DEPTH, N_EXPERTS, d), 0.02),
        "ffn_ln_g": 1.0 + nrm((DEPTH, d), 0.02),
        "ffn_ln_b": nrm((DEPTH, d), 0.02),
    }

def reference(x, pool_w, pool_scale, sc_w_in, sc_conv_w, sc_w_out,
              cf_w_in, cf_b_in, cf_dw_w, cf_dw_b, cf_ln_g, cf_ln_b, cf_w_out, cf_b_out,
              mix_ln_g, mix_ln_b, router_w, router_b, moe_w_gu, moe_b_gu, moe_w_dn, moe_b_dn,
              ffn_ln_g, ffn_ln_b):
    ia, ib, ic = 0, 0, 0
    for layer in range(DEPTH):
        kind = layer % N_MIXERS
        if kind == 0:
            h = pool_mixer(x, pool_w[ia], pool_scale[ia])
            ia += 1
        elif kind == 1:
            h = short_conv_mixer(x, sc_w_in[ib], sc_conv_w[ib], sc_w_out[ib])
            ib += 1
        else:
            h = conformer_conv_mixer(x, cf_w_in[ic], cf_b_in[ic], cf_dw_w[ic], cf_dw_b[ic],
                                     cf_ln_g[ic], cf_ln_b[ic], cf_w_out[ic], cf_b_out[ic])
            ic += 1
        x = layer_norm(DEEPNORM_ALPHA * x + h, mix_ln_g[layer], mix_ln_b[layer])
        h = moe_ffn(x, router_w[layer], router_b[layer], moe_w_gu[layer], moe_b_gu[layer],
                    moe_w_dn[layer], moe_b_dn[layer])
        x = layer_norm(DEEPNORM_ALPHA * x + h, ffn_ln_g[layer], ffn_ln_b[layer])
    return x


_drawn_inputs = setup_inputs


def setup_inputs(seed=0):
    import zlib

    import numpy as np

    out = dict(_drawn_inputs(seed))
    spreads = {}
    factors = {'router_b': 3.529,
     'moe_b_gu': 8.0,
     'moe_b_dn': 6.427,
     'ffn_ln_g': 2.813,
     'ffn_ln_b': 2.909}
    for name, (base, spread) in spreads.items():
        noise = np.random.default_rng([zlib.crc32(name.encode()), seed]).standard_normal(out[name].shape)
        drawn = base * np.exp(spread * noise) if base else spread * noise
        out[name] = jnp.asarray(drawn.astype(out[name].dtype))
    for name, factor in factors.items():
        out[name] = (out[name] * factor).astype(out[name].dtype)
    return out
```

```python
import concourse.bass as bass
from concourse import mybir
from contextlib import ExitStack

F32 = mybir.dt.float32
F32R = mybir.dt.float32r
BF16 = mybir.dt.bfloat16
I32 = mybir.dt.int32
ALU = mybir.AluOpType
ACT = mybir.ActivationFunctionType
AX = mybir.AxisListType

P = 128
D = 1024
SEQ = 1024
KD = D // P
NT = SEQ // P
GROUPS = 4
WINDOWS = (2, 4, 8, 16)
REACH = 16
EXPERTS = 32
TOPK = 4
SLOTS = 160
TAIL = SLOTS - P
MORE = -(-SEQ // SLOTS) - 1
OVER = TOPK * SEQ // SLOTS
JOBS = EXPERTS + OVER
TABLE = 64
ALPHA = 2.0 ** 0.25
EPS = 1e-5
LIMIT = 7.0
SWIGLU = 1.702
FAR = 4096.0

GU = 8
DN = 4
UNITS = GU + DN
COLS = 256
LOADS = UNITS // 2
RAWS = 3
RING = 4
TILES = 2 * UNITS
HI_AHEAD, LO_AHEAD = 3, 2
POOL_LO = (3, 6, 11)

POOL_STEPS = 10

K_IDENT, K_IOTA, K_JUNK, K_BOFF = 0, P, P + SLOTS, P + SLOTS + 2
K_END = K_BOFF + MORE + 1
C_BAND, C_FIRST, C_PREV = 0, GROUPS * P, 2 * GROUPS * P
C_TRI = C_PREV + GROUPS * REACH
C_SEG = C_TRI + P
C_LEVEL = C_SEG + NT * EXPERTS
C_ECODE = C_LEVEL + EXPERTS * MORE
C_BCODE = C_ECODE + EXPERTS * MORE
C_PIDX = C_BCODE + EXPERTS * MORE
C_TOK = C_PIDX + 1
C_END = C_TOK + 3 * NT


def pool_n(job, n):
    return job * POOL_STEPS + n


def lo_count(pool, job, unit):
    own = [u for u in range(UNITS) if (u in POOL_LO) == pool]
    return job * len(own) + len([u for u in own if u <= unit])


def build_program(nc, x, w_mix, mix_scale, ln1, ln2, router_w, router_b, w_gu, w_dn, biases, keep, consts,
                  table0, out):
    x1_rows = nc.dram_tensor("x1_rows", [SEQ + SLOTS, D], F32).ap()
    sum_rows = nc.dram_tensor("sum_rows", [SEQ + SLOTS, D], F32).ap()

    ctx = ExitStack()
    with ctx:
        def sb(name, shape, dt=F32):
            return ctx.enter_context(nc.sbuf_tensor(name, shape, dt))

        def sem(name):
            return ctx.enter_context(nc.semaphore(name))

        region = 2 * RING * KD * COLS * 4
        sb("region", [P, region // 4])
        region_at = nc.sbuf_base - region

        raw = sb("raw", [P, RAWS, KD, 2 * COLS])
        x_rows = sb("x_rows", [P, 2, D])
        x_parts = sb("x_parts", [P, KD, 2, SLOTS], F32R)
        act = sb("act", [P, KD, SLOTS])
        act_parts = sb("act_parts", [P, KD, 2, SLOTS], F32R)
        half = sb("half", [P, 2, 2, SLOTS])
        inner = sb("inner", [P, 2, 2, SLOTS])
        sig = sb("sig", [P, 2, SLOTS])
        up_gate = sb("up_gate", [P, 2, SLOTS])
        y_cols = sb("y_cols", [P, 2, 2, 2 * P])
        y_rows = sb("y_rows", [P, 2, D])
        onehot = sb("onehot", [P, NT, 2 * P], BF16)
        slot_src = sb("slot_src", [P, NT, 6], BF16)
        slot_val = sb("slot_val", [P, 2, 6])
        rank_col = sb("rank_col", [P, NT])
        tiny = sb("tiny", [P, 5, 2])
        idx_next = sb("idx_next", [P, 2], I32)
        idx_cur = sb("idx_cur", [P, 2], I32)
        gate_next = sb("gate_next", [P, 2])
        gate_cur = sb("gate_cur", [P, 2])
        bias_next = sb("bias_next", [P, 3 * KD])
        bias_cur = sb("bias_cur", [P, 3 * KD])
        rank = sb("rank", [P, NT, EXPERTS])
        gate3 = sb("gate3", [P, NT, EXPERTS, 3], BF16)
        kc = sb("kc", [P, K_END])
        table = sb("table", [1, 2, TABLE], I32)
        ident = kc[:, K_IDENT:K_IDENT + P]

        cc = sb("cc", [P, C_END])
        x1_t = sb("x1_t", [P, 2, D])
        gb1 = sb("gb1", [P, 2, D])
        rw = sb("rw", [P, KD, EXPERTS])
        rb = sb("rb", [P, EXPERTS])
        tri = sb("tri", [P, 2, P], BF16)
        mv = sb("mv", [P, 2, 18])
        sum_t = y_rows

        def place(name, shape, dt, offset):
            size = 4
            for n in shape[1:]:
                size *= n
            assert offset + size <= region
            return nc.alloc_sbuf_tensor_at(name, shape, dt, offset=region_at + offset)

        w_hi = place("w_hi", [P, RING, KD, 2, P], F32R, 0)
        w_lo = place("w_lo", [P, RING, KD, 2, P], F32R, region // 2)
        kb = 1024
        x_t = place("x_t", [P, NT, D], F32, 0)
        wm = place("wm", [P, KD, 2 * P], F32, 32 * kb)
        diff = place("diff", [P, KD, P], F32, 40 * kb)
        res = place("res", [P, 2, D], F32, 44 * kb)
        x1_cols = place("x1_cols", [P, KD, P], F32, 52 * kb)
        scale_b = place("scale_b", [P, D], F32, 56 * kb)
        fin = place("fin", [P, NT, D], F32, 0)
        gb2 = place("gb2", [P, 2, D], F32, 32 * kb)

        lg, big, eq, cs, sel, ex = (place(n, [P, NT, EXPERTS], F32, (56 + i) * kb)
                                    for i, n in enumerate(("lg", "big", "eq", "cs", "sel", "ex")))
        top = sb("top", [P, NT, 8])
        per = sb("per", [P, 4, NT])
        mask = sb("mask", [P, NT, EXPERTS], BF16)
        cnt = sb("cnt", [P, EXPERTS])
        fl = sb("fl", [P, EXPERTS, MORE])
        ps_ = sb("ps_", [P, EXPERTS, MORE])
        pt = sb("pt", [P, EXPERTS, MORE])
        code = sb("code", [P, 3])

        pair = [ctx.enter_context(nc.psum_tensor(f"pair{i}", [P, 2, 512], F32)) for i in range(4)]
        bank = [p[:, i] for p in pair for i in range(2)]
        unit_banks, ub, tb, dispatch_bank, rank_bank = pair[0:2], bank[0:4], bank[4:6], bank[6], bank[7]

        s_kc, s_wm, s_gb, s_rw = sem("s_kc"), sem("s_wm"), sem("s_gb"), sem("s_rw")
        s_x = [sem(f"s_x_tile{i}") for i in range(NT)]
        s_scaled = sem("s_scaled")
        s_diff = sem("s_diff")
        s_diffc = sem("s_diffc")
        s_h = sem("s_h")
        s_res = sem("s_res")
        s_dve = sem("s_dve")
        s_var = sem("s_var")
        s_std = sem("s_std")
        s_nrm = sem("s_nrm")
        s_xn = sem("s_xn")
        s_gx = sem("s_gx")
        s_x1 = sem("s_x1")
        s_ax = sem("s_ax")
        s_st = [sem(f"s_st{i}") for i in range(2)]
        s_tr = sem("s_tr")
        s_trc = [sem("s_trc_act"), sem("s_trc_dve")]
        s_lg = sem("s_lg")
        s_ex = sem("s_ex")
        s_mask = sem("s_mask")
        s_rank = sem("s_rank")
        s_route = sem("s_route")
        s_code = sem("s_code")
        s_row = sem("s_row")
        s_tab0, s_tab = sem("s_tab0"), sem("s_tab")
        s_zero = sem("s_zero")
        s_apart = sem("s_apart")
        s_init = sem("s_init")

        s_raw = [sem(f"s_raw{i}") for i in range(RAWS)]
        s_hi = sem("s_hi")
        s_lo = [sem("s_lo_dve"), sem("s_lo_pool")]
        s_tile = sem("s_tile")
        s_half = sem("s_half")
        s_out_of = sem("s_out_of")
        s_in = sem("s_in")
        s_ug = sem("s_ug")
        s_sig = sem("s_sig")
        s_act = sem("s_act")
        s_ahi, s_alo = sem("s_ahi"), sem("s_alo")
        s_ytr = sem("s_ytr")
        s_yrow = sem("s_yrow")
        s_col = sem("s_col")
        s_hot = sem("s_hot")
        s_disp = sem("s_disp")
        s_val = sem("s_val")
        s_pool = sem("s_pool")
        s_gat = [sem("s_gat_main"), sem("s_gat_tail")]
        s_xtr = sem("s_xtr")
        s_xhi, s_xlo = sem("s_xhi"), sem("s_xlo")
        s_bias, s_bcur = sem("s_bias"), sem("s_bcur")
        s_sum = [sem("s_sum_main"), sem("s_sum_tail")]
        s_fin = [sem(f"s_fin{i}") for i in range(NT)]
        s_gb2, s_out = sem("s_gb2"), sem("s_out")

        block = ctx.enter_context(nc.Block())

        def wait(eng, s, value):
            if not isinstance(value, int) or value > 0:
                eng.wait_ge(s, value)

        def apart(eng):
            eng.sem_inc(s_apart, 1)

        def of(job, unit):
            return (job + 1, unit - UNITS) if unit >= UNITS else (job, unit)

        def tile_n(j, u, t):
            return j * TILES + 2 * u + t + 1

        def out_of(j, u):
            return j * UNITS + 2 + u + 1

        def turned(q):
            return tb[q % 2].rearrange("p (k s) -> p k s", k=2)[:, :, 0:SLOTS]

        def wait_raw(eng, job, unit):
            load = unit // 2
            eng.wait_ge(s_raw[load % RAWS], (job * (LOADS // RAWS) + load // RAWS + 1) * 16)

        def wait_lo(eng, job, unit):
            pool = unit in POOL_LO
            eng.wait_ge(s_lo[pool], lo_count(pool, job, unit))

        def unit_of_raw(t, unit):
            v = t[:, unit // 2 % RAWS, :, unit % 2 * COLS:(unit % 2 + 1) * COLS]
            if unit < GU:
                return v.rearrange("p k (n t) -> p k t n", t=2)
            return v.rearrange("p k (t n) -> p k t n", t=2)

        def lo_part(eng, job, unit):
            eng.wait_ge(s_hi, job * UNITS + unit + 1)
            r = unit % RING
            eng.tensor_tensor(w_lo[:, r], unit_of_raw(raw, unit), w_hi[:, r].bitcast(F32), ALU.subtract)\
               .then_inc(s_lo[unit in POOL_LO], 1)

        @block.sync
        def _(sp):
            def load_weights(e, load):
                slot = load % RAWS
                if load < GU // 2:
                    src = w_gu[e, :, load * 2 * COLS:(load + 1) * 2 * COLS]
                else:
                    src = w_dn[e, :, (load - GU // 2) * 2 * COLS:(load - GU // 2 + 1) * 2 * COLS]
                sp.dma_start(raw[:, slot], src.rearrange("(k p) n -> p k n", p=P)).then_inc(s_raw[slot], 16)

            sp.dma_start(x_t[:, 0], x[0:P, :]).then_inc(s_x[0], 16)
            sp.dma_start(cc[:, :], consts).then_inc(s_kc, 16)
            sp.dma_start(wm[:, :, :], w_mix.rearrange("(k p) n -> p k n", p=P)).then_inc(s_wm, 16)
            sp.dma_start(scale_b[:, :], mix_scale.to_broadcast((P, D))).then_inc(s_wm, 16)
            sp.dma_start(kc[:, :], keep).then_inc(s_kc, 16)
            sp.dma_start(x_t[:, 1], x[P:2 * P, :]).then_inc(s_x[1], 16)
            for i in range(2):
                sp.dma_start(gb1[:, i], ln1[i:i + 1, :].to_broadcast((P, D))).then_inc(s_gb, 16)
            sp.dma_start(rw[:, :, :], router_w.rearrange("(k p) n -> p k n", p=P)).then_inc(s_rw, 16)
            sp.dma_start(rb[:, :], router_b.to_broadcast((P, EXPERTS))).then_inc(s_rw, 16)
            sp.dma_start(table[:, :, :], table0).then_inc(s_tab0, 16)
            for i in range(2, NT):
                sp.dma_start(x_t[:, i], x[i * P:(i + 1) * P, :]).then_inc(s_x[i], 16)
            sp.wait_ge(s_zero, 1)
            zeros = x_rows[:, 1]
            sp.dma_start(x1_rows[SEQ:SEQ + P, :], zeros).then_inc(s_gb2, 16)
            sp.dma_start(x1_rows[SEQ + P:SEQ + SLOTS, :], zeros[0:TAIL]).then_inc(s_gb2, 16)
            for load in range(RAWS):
                load_weights(0, load)
            sp.dma_start(bias_next[:, :], biases[0]).then_inc(s_bias, 16)
            for i in range(NT):
                sp.wait_ge(s_x1, i + 1)
                sp.dma_start(x1_rows[i * P:(i + 1) * P, :], x1_t[:, i % 2]).then_inc(s_st[i % 2], 16)
                sp.wait_ge(s_ax, i + 1)
                sp.dma_start(sum_rows[i * P:(i + 1) * P, :], sum_t[:, i % 2]).then_inc(s_st[i % 2], 16)
            sp.wait_ge(s_tab, 2)
            jobs = sp.value_load(table[0:1, 0, TABLE - 1:TABLE], min_val=EXPERTS, max_val=JOBS)
            with sp.Fori(0, jobs) as j:
                for q in range(LOADS):
                    if q % RAWS == 0:
                        nxt = q // RAWS
                        e = sp.value_load(table[0:1, 0, bass.ds(j + nxt, 1)], min_val=0, max_val=EXPERTS - 1)
                    for unit in (2 * q, 2 * q + 1):
                        wait_lo(sp, j, unit)
                        apart(sp)
                    load_weights(e, (q + RAWS) % LOADS)
                    if q == RAWS:
                        sp.wait_ge(s_bcur, j * 3 + 3)
                        apart(sp)
                        sp.dma_start(bias_next[:, :], biases[e]).then_inc(s_bias, 16)
            for s in s_sum:
                sp.wait_ge(s, jobs * 16 + 16)
            sp.wait_ge(s_hi, jobs * UNITS + HI_AHEAD)
            apart(sp)
            sp.wait_ge(s_lo[0], lo_count(False, jobs, LO_AHEAD - 1))
            apart(sp)
            sp.wait_ge(s_tile, jobs * TILES)
            apart(sp)
            for i in range(NT):
                sp.dma_start(fin[:, i], sum_rows[i * P:(i + 1) * P, :]).then_inc(s_fin[i], 16)
                if i < 2:
                    sp.dma_start(gb2[:, i], ln2[i:i + 1, :].to_broadcast((P, D))).then_inc(s_gb2, 16)
            for i in range(NT):
                sp.wait_ge(s_x1, NT + i + 1)
                sp.dma_start(out[i * P:(i + 1) * P, :], fin[:, i]).then_inc(s_out, 16)
            sp.wait_ge(s_out, 16 * NT)
            for i in range(RAWS):
                sp.wait_ge(s_raw[i], jobs * (LOADS // RAWS) * 16 + 16)
            sp.wait_ge(s_bias, jobs * 16 + 16)
            apart(sp)

        @block.tensor
        def _(pe):
            def mix(i):
                pe.wait_ge(s_x[i], 16)
                for half in range(2):
                    if i > 0:
                        pe.wait_ge(s_diffc, 2 * i - 1 + half)
                    for c in range(4 * half, 4 * half + 4):
                        g = c // 2
                        o = ub[half][:, c % 4 * P:(c % 4 + 1) * P]
                        cols = slice(c * P, (c + 1) * P)
                        b = (C_FIRST if i == 0 else C_BAND) + g * P
                        last = pe.matmul(o, x_t[:, i, cols], cc[:, b:b + P], start=True, stop=i == 0)
                        if i > 0:
                            b = C_PREV + g * REACH
                            last = pe.matmul(o[:, 0:REACH], x_t[:, i - 1, cols], cc[:, b:b + REACH],
                                             start=False, stop=True)
                    last.then_inc(s_diff, 1)
                for half in range(2):
                    pe.wait_ge(s_diffc, 2 * i + half + 1)
                    if i > 0:
                        pe.wait_ge(s_res, 2 * i - 1 + half)
                    for g in (2 * half, 2 * half + 1):
                        for k in range(2):
                            last = pe.matmul(ub[2 + half][:, g % 2 * 256:(g % 2 + 1) * 256],
                                             diff[:, 2 * g + k], wm[:, 2 * g + k], start=k == 0, stop=k == 1)
                    last.then_inc(s_h, 1)

            def route(i):
                pe.wait_ge(s_x1, i + 1)
                for half in range(2):
                    if i > 0:
                        pe.wait_ge(s_trc[half], i)
                    for c in range(4):
                        k = 4 * half + c
                        last = pe.transpose(tb[half][:, c * P:(c + 1) * P], x1_t[:, i % 2, k * P:(k + 1) * P], ident)
                    last.then_inc(s_tr, 1)
                for k in range(KD):
                    if k % 4 == 0:
                        pe.wait_ge(s_trc[k // 4], i + 1)
                    last = pe.matmul(dispatch_bank[:, i * EXPERTS:(i + 1) * EXPERTS], x1_cols[:, k], rw[:, k],
                                     start=k == 0, stop=k == KD - 1)
                last.then_inc(s_lg, 1)

            pe.wait_ge(s_kc, 32)
            pe.wait_ge(s_scaled, 1)
            pe.wait_ge(s_rw, 32)
            for i in range(NT + 2):
                if i < NT:
                    mix(i)
                if i >= 2:
                    route(i - 2)
            pe.wait_ge(s_zero, 6)
            pe.wait_ge(s_mask, 1)
            r = rank_bank[:, 0:NT * EXPERTS]
            pe.matmul(r, tri[:, 0], mask[:, :, :].rearrange("p a b -> p (a b)"), start=True, stop=False)
            for i in range(NT - 1):
                o = rank_bank[:, (i + 1) * EXPERTS:NT * EXPERTS]
                pe.matmul(o, tri[:, 1], mask[:, i:i + 1].to_broadcast((P, NT - 1 - i, EXPERTS)),
                          start=False, stop=i == NT - 2)
            for i in range(NT):
                last = pe.matmul(rank_bank[:, 256:256 + EXPERTS], tri[:, 1], mask[:, i], start=i == 0, stop=i == NT - 1,
                                 skip_group_check=True)
            last.then_inc(s_rank, 1)

            def dispatch(job):
                pe.wait_ge(s_hot, job + 1)
                wait(pe, s_val, job)
                for part in range(2):
                    for i in range(NT):
                        last = pe.matmul(dispatch_bank[:, 8 * part:8 * part + 6], onehot[:, i, part * P:(part + 1) * P],
                                         slot_src[:, i], start=i == 0, stop=i == NT - 1)
                last.then_inc(s_disp, 1)

            def turn_x(job, q):
                if q == 0:
                    for s in s_gat:
                        pe.wait_ge(s, job * 16 + 16)
                    if not isinstance(job, int):
                        pe.wait_ge(s_yrow, job * 4 - 3)
                if q >= 2:
                    pe.wait_ge(s_xlo, job * 4 + q - 1)
                for k in (2 * q, 2 * q + 1):
                    for part in range(2):
                        o = k % 2 * 2 * P + part * P
                        last = pe.transpose(tb[q % 2][:, o:o + P], x_rows[:, part, k * P:(k + 1) * P], ident)
                last.then_inc(s_xtr, 1)

            def turn_y(j, i):
                pe.wait_ge(s_out_of, out_of(j, GU + i))
                if i == 0:
                    pe.wait_ge(s_xlo, j * 4 + 8)
                if i == 2:
                    pe.wait_ge(s_yrow, j * 4 + 3)
                for t in range(2):
                    c = (2 * i + t) % 4 * P
                    for part in range(2):
                        last = pe.transpose(tb[part][:, c:c + P], y_cols[:, i % 2, t, part * P:(part + 1) * P], ident)
                last.then_inc(s_ytr, 1)

            def products(j, u):
                pe.wait_ge(s_hi, j * UNITS + u + 1)
                wait_lo(pe, j, u)
                if u == 0:
                    pe.wait_ge(s_xlo, j * 4 + 4)
                parts = x_parts if u < GU else act_parts
                r = u % RING
                pe.wait_ge(s_out_of, out_of(j, u - 2))
                for t in range(2):
                    o = ub[u % 2 * 2 + t]
                    for k in range(KD):
                        if u == GU and t == 0 and k in (0, KD - 1):
                            n = j * GU + (KD - 1 if k == 0 else KD)
                            pe.wait_ge(s_ahi, n)
                            pe.wait_ge(s_alo, n)
                        for lo in ((0, 1) if k == 0 else (1, 0)):
                            if lo:
                                pe.matmul(o[:, SLOTS:2 * SLOTS], w_lo[:, r, k, t], parts[:, k, 0],
                                          start=False, stop=False)
                            else:
                                last = pe.matmul(o[:, 0:2 * SLOTS], w_hi[:, r, k, t],
                                                 parts[:, k].rearrange("p a b -> p (a b)"),
                                                 start=k == 0, stop=k == KD - 1)
                    last.then_inc(s_tile, 1)

            pe.wait_ge(s_route, 1)
            pe.wait_ge(s_res, 2 * NT)
            pe.wait_ge(s_diffc, 2 * NT)
            dispatch(0)
            pe.wait_ge(s_code, 1)
            for n in range(2):
                last = pe.matmul(rank_bank[0:1, n * P:(n + 1) * P], code[:, n:n + 1], ident, start=True, stop=True)
            last.then_inc(s_row, 1)
            for q in range(4):
                turn_x(0, q)
            pe.wait_ge(s_tab, 2)
            jobs = pe.value_load(table[0:1, 0, TABLE - 1:TABLE], min_val=EXPERTS, max_val=JOBS)
            with pe.Fori(0, jobs) as j:
                for u in range(UNITS):
                    products(j, u)
                    if u == 2:
                        dispatch(j + 1)
                    if u in (GU - 1, GU):
                        turn_x(j + 1, 2 * (u - GU + 1))
                        turn_x(j + 1, 2 * (u - GU + 1) + 1)
                    if u > GU:
                        turn_y(j, u - GU - 1)
                turn_y(j, DN - 1)

        @block.scalar
        def _(ac):
            def hi_part(job, unit):
                wait_raw(ac, job, unit)
                ac.activation(w_hi[:, unit % RING], unit_of_raw(raw, unit), ACT.Copy).then_inc(s_hi, 1)

            def copy_diff(i):
                for half in range(2):
                    ac.wait_ge(s_diff, 2 * i + half + 1)
                    if i > 0:
                        ac.wait_ge(s_h, 2 * i - 1 + half)
                    ac.activation(diff[:, 4 * half:4 * half + 4].rearrange("p a b -> p (a b)"), ub[half],
                                  ACT.Copy).then_inc(s_diffc, 1)

            def normalise(n, src):
                ac.wait_ge(s_var, n + 1)
                m = mv[:, n % 2]
                ac.activation(m[:, 15:16], m[:, 14:15], ACT.Sqrt).then_inc(s_std, 1)
                ac.wait_ge(s_nrm, n + 1)
                ac.activation(src, src, ACT.Identity, scale=m[:, 16:17], bias=m[:, 17:18]).then_inc(s_xn, 1)

            def store_sum(i):
                ac.wait_ge(s_x1, i + 1)
                if i >= 2:
                    ac.wait_ge(s_st[i % 2], i // 2 * 32)
                ac.activation(sum_t[:, i % 2], x1_t[:, i % 2], ACT.Copy, scale=ALPHA).then_inc(s_ax, 1)

            def copy_x1(i):
                ac.wait_ge(s_tr, 2 * i + 1)
                if i > 0:
                    ac.wait_ge(s_lg, i)
                ac.activation(x1_cols[:, 0:4].rearrange("p a b -> p (a b)"), tb[0], ACT.Copy)\
                  .then_inc(s_trc[0], 1)

            for i in range(NT + 2):
                if i < NT:
                    copy_diff(i)
                if 1 <= i <= NT:
                    normalise(i - 1, res[:, (i - 1) % 2])
                if i >= 2:
                    store_sum(i - 2)
                    copy_x1(i - 2)
            ac.wait_ge(s_ex, 1)
            ac.activation(ex[:, :, :], ex[:, :, :], ACT.Exp).then_inc(s_ex, 1)
            ac.wait_ge(s_x1, NT)
            ac.wait_ge(s_lg, NT)
            for unit in range(HI_AHEAD):
                hi_part(0, unit)

            def copy_x(job, q):
                ac.wait_ge(s_xtr, job * 4 + q + 1)
                ac.activation(x_parts[:, 2 * q:2 * q + 2, 0], turned(q), ACT.Copy).then_inc(s_xhi, 1)

            def y_out(j, half):
                ac.wait_ge(s_ytr, j * 4 + 2 * half + 2)
                if half == 0:
                    ac.wait_ge(s_pool, pool_n(j + 1, 3))
                cols = slice(half * 512, half * 512 + 512)
                for part, rows in ((0, P), (1, TAIL)):
                    if half == 0:
                        ac.wait_ge(s_sum[part], j * 16 + 16)
                    ac.activation(y_rows[0:rows, part, cols], tb[part][0:rows, :], ACT.Copy,
                                  scale=gate_cur[0:rows, part:part + 1]).then_inc(s_yrow, 1)

            for q in range(4):
                copy_x(0, q)
            for s in s_st:
                ac.wait_ge(s, NT // 2 * 32)
            ac.activation(tiny[:, 3, 0:1], kc[:, 0:1], ACT.Copy).then_inc(s_yrow, 1)
            ac.wait_ge(s_tab, 2)
            jobs = ac.value_load(table[0:1, 0, TABLE - 1:TABLE], min_val=EXPERTS, max_val=JOBS)
            with ac.Fori(0, jobs) as j:
                def split_act(u):
                    ac.wait_ge(s_act, j * GU + u + 1)
                    ac.activation(act_parts[:, u, 0], act[:, u], ACT.Copy).then_inc(s_ahi, 1)

                def second_half(u, t):
                    ac.wait_ge(s_tile, tile_n(j, u, t))
                    b = t * KD + u if u < GU else 2 * KD + 2 * (u - GU) + t
                    ac.activation(half[:, u % 2, t], ub[u % 2 * 2 + t][:, SLOTS:2 * SLOTS],
                                  ACT.Identity, bias=bias_cur[:, b:b + 1]).then_inc(s_half, 1)

                ac.activation(tiny[:, 3, 1:2], kc[:, 0:1], ACT.Sigmoid)
                ac.wait_ge(s_bcur, j * 3 + 3)
                for u in range(UNITS):
                    hi_part(*of(j, u + HI_AHEAD))
                    if 0 < u < GU:
                        split_act(u - 1)
                    if u == GU:
                        copy_x(j + 1, 0)
                        copy_x(j + 1, 1)
                    second_half(u, 0)
                    second_half(u, 1)
                    if u < GU:
                        ac.wait_ge(s_in, j * 2 * GU + 2 * u + 1)
                        ac.activation(sig[:, u % 2], inner[:, u % 2, 0], ACT.Sigmoid, scale=SWIGLU).then_inc(s_sig, 1)
                    if u == GU - 1:
                        split_act(u)
                    if u == GU:
                        copy_x(j + 1, 2)
                        copy_x(j + 1, 3)
                    if u == UNITS - 1:
                        y_out(j, 0)
                        y_out(j, 1)
            for i in range(NT):
                normalise(NT + i, fin[:, i])

        @block.vector
        def _(ve):
            done = [0]

            def then_wait(ins):
                done[0] += 1
                ins.then_inc(s_dve, 1)
                ve.wait_ge(s_dve, done[0])

            def norm_stats(n, halves):
                m = mv[:, n % 2]
                for half in range(2):
                    last = ve.bn_stats(m[:, 6 * half:6 * half + 6], halves[half])
                    then_wait(last)
                then_wait(ve.bn_aggr(m[:, 12:14], m[:, 0:12]))
                ve.tensor_scalar(m[:, 14:15], m[:, 13:14], EPS, None, ALU.add).then_inc(s_var, 1)

            def norm_scale(n):
                m = mv[:, n % 2]
                ve.wait_ge(s_std, n + 1)
                then_wait(ve.reciprocal(m[:, 16:17], m[:, 15:16]))
                ve.tensor_scalar(m[:, 17:18], m[:, 12:13], m[:, 16:17], -1.0, ALU.mult, ALU.mult).then_inc(s_nrm, 1)

            ve.memset(x_rows[:, 1], 0.0).then_inc(s_zero, 1)
            ve.memset(onehot[:, :, :], 0.0).then_inc(s_zero, 1)
            ve.memset(y_cols[:, :, :, :], 0.0).then_inc(s_zero, 1)
            ve.wait_ge(s_wm, 32)
            ve.tensor_tensor(wm[:, :, :].rearrange("p (g k) n -> p g k n", k=2),
                             wm[:, :, :].rearrange("p (g k) n -> p g k n", k=2),
                             scale_b[:, :].rearrange("p (g o n) -> p g o n", g=GROUPS, o=1)
                             .to_broadcast((P, GROUPS, 2, 256)), ALU.mult).then_inc(s_scaled, 1)
            ve.wait_ge(s_kc, 32)
            ve.tensor_copy(tri[:, 0], cc[:, C_TRI:C_TRI + P]).then_inc(s_zero, 1)
            ve.memset(tri[:, 1], 1.0).then_inc(s_zero, 1)
            ve.tensor_copy(slot_src[:, :, 0:3],
                           cc[:, C_TOK:C_TOK + 3 * NT].rearrange("p (i c) -> p i c", c=3)).then_inc(s_zero, 1)
            ve.wait_ge(s_gb, 32)

            def residual(i):
                ve.wait_ge(s_x[i], 16)
                if i >= 2:
                    ve.wait_ge(s_gx, i - 1)
                for half in range(2):
                    ve.wait_ge(s_h, 2 * i + half + 1)
                    cols = slice(half * 512, half * 512 + 512)
                    ve.scalar_tensor_tensor(res[:, i % 2, cols], x_t[:, i, cols], ALPHA, ub[2 + half],
                                            ALU.mult, ALU.add).then_inc(s_res, 1)
                ve.wait_ge(s_res, 2 * i + 2)
                norm_stats(i, [res[:, i % 2, 0:512], res[:, i % 2, 512:1024]])

            def times_g(i):
                norm_scale(i)
                ve.wait_ge(s_xn, i + 1)
                if i >= 2:
                    ve.wait_ge(s_st[i % 2], i // 2 * 32)
                    ve.wait_ge(s_tr, 2 * i - 2)
                    ve.wait_ge(s_ax, i - 1)
                ve.tensor_tensor(x1_t[:, i % 2], res[:, i % 2], gb1[:, 0], ALU.mult).then_inc(s_gx, 1)

            def copy_x1(i):
                ve.wait_ge(s_tr, 2 * i + 2)
                if i > 0:
                    ve.wait_ge(s_lg, i)
                ve.tensor_copy(x1_cols[:, 4:8].rearrange("p a b -> p (a b)"), tb[1]).then_inc(s_trc[1], 1)

            for i in range(NT + 2):
                if i < NT:
                    residual(i)
                if 1 <= i <= NT:
                    times_g(i - 1)
                if i >= 2:
                    copy_x1(i - 2)

            ve.wait_ge(s_lg, NT)
            ve.wait_ge(s_rw, 32)
            flat = dispatch_bank[:, 0:NT * EXPERTS].rearrange("p (i e) -> p i e", e=EXPERTS)
            whole = (P, NT, EXPERTS)
            then_wait(ve.tensor_tensor(lg[:, :, :], flat, rb[:, :].rearrange("p (o e) -> p o e", o=1).to_broadcast(whole),
                                       ALU.add))
            for i in range(NT):
                last = ve.max(top[:, i], lg[:, i])
            then_wait(last)
            fourth = top[:, :, TOPK - 1:TOPK].to_broadcast(whole)
            ve.tensor_tensor(ex[:, :, :], lg[:, :, :], top[:, :, 0:1].to_broadcast(whole), ALU.subtract).then_inc(s_ex, 1)
            then_wait(ve.tensor_tensor(big[:, :, :], lg[:, :, :], fourth, ALU.is_gt))
            then_wait(ve.tensor_tensor(eq[:, :, :], lg[:, :, :], fourth, ALU.is_equal))
            then_wait(ve.tensor_reduce(per[:, 0], big[:, :, :], AX.X, ALU.add))
            then_wait(ve.tensor_scalar(per[:, 1], per[:, 0], -1.0, float(TOPK), ALU.mult, ALU.add))
            line = lambda t: t[:, :, :].rearrange("p i e -> p (i e)")
            then_wait(ve.tensor_tensor_scan(line(cs), cc[:, C_SEG:C_SEG + NT * EXPERTS], line(eq), 0.0, ALU.mult, ALU.add))
            then_wait(ve.tensor_tensor(cs[:, :, :], cs[:, :, :],
                                       per[:, 1].rearrange("p (i o) -> p i o", o=1).to_broadcast(whole), ALU.is_le))
            then_wait(ve.tensor_tensor(cs[:, :, :], cs[:, :, :], eq[:, :, :], ALU.mult))
            then_wait(ve.tensor_tensor(sel[:, :, :], cs[:, :, :], big[:, :, :], ALU.add))
            ve.tensor_copy(mask[:, :, :], sel[:, :, :]).then_inc(s_mask, 1)
            ve.wait_ge(s_ex, 2)
            then_wait(ve.tensor_tensor(ex[:, :, :], ex[:, :, :], sel[:, :, :], ALU.mult))
            then_wait(ve.tensor_reduce(per[:, 2], ex[:, :, :], AX.X, ALU.add))
            then_wait(ve.reciprocal(per[:, 3], per[:, 2]))
            then_wait(ve.tensor_tensor(ex[:, :, :], ex[:, :, :],
                                       per[:, 3].rearrange("p (i o) -> p i o", o=1).to_broadcast(whole), ALU.mult))
            part = lambda n: gate3[:, :, :, n:n + 1].rearrange("p i e o -> p i (e o)")
            for n in range(2):
                then_wait(ve.tensor_copy(part(n), ex[:, :, :]))
                then_wait(ve.tensor_tensor(ex[:, :, :], ex[:, :, :], part(n), ALU.subtract))
            then_wait(ve.tensor_copy(part(2), ex[:, :, :]))
            then_wait(ve.tensor_scalar(sel[:, :, :], sel[:, :, :], -FAR, FAR, ALU.mult, ALU.add))
            ve.wait_ge(s_rank, 1)
            then_wait(ve.tensor_tensor(rank[:, :, :], sel[:, :, :],
                                       rank_bank[:, 0:NT * EXPERTS].rearrange("p (i e) -> p i e", e=EXPERTS), ALU.add))
            then_wait(ve.tensor_copy(cnt[:, :], rank_bank[:, 256:256 + EXPERTS]))
            ve.tensor_copy(per[:, 0, 0:1], rank[:, 0, 0:1]).then_inc(s_route, 1)

            def hot(job):
                ve.wait_ge(s_col, job + 1)
                if not (isinstance(job, int) and job == 0):
                    ve.wait_ge(s_disp, job)
                shape = (P, NT, SLOTS)
                ve.tensor_tensor(onehot[:, :, 0:SLOTS],
                                 rank_col[:, :].rearrange("p (i o) -> p i o", o=1).to_broadcast(shape),
                                 kc[:, K_IOTA:K_IOTA + SLOTS].rearrange("p (o s) -> p o s", o=1).to_broadcast(shape),
                                 ALU.is_equal).then_inc(s_hot, 1)

            def slot_values(job):
                ve.wait_ge(s_disp, job + 1)
                if not (isinstance(job, int) and job == 0):
                    ve.wait_ge(s_pool, pool_n(job - 1, 9))
                ve.tensor_copy(slot_val[:, :, :],
                               dispatch_bank[:, 0:16].rearrange("p (c n) -> p c n", n=8)[:, :, 0:6]).then_inc(s_val, 1)

            def x_lo_part(job, q):
                ve.wait_ge(s_xhi, job * 4 + q + 1)
                k = slice(2 * q, 2 * q + 2)
                ve.tensor_tensor(x_parts[:, k, 1], turned(q), x_parts[:, k, 0].bitcast(F32), ALU.subtract)\
                  .then_inc(s_xlo, 1)

            ve.tensor_copy(tiny[:, 4, 0:1], kc[:, 0:1]).then_inc(s_out_of, 2)
            hot(0)
            levels = (P, EXPERTS, MORE)
            fl_, po_, pt_ = (t[:, :, :].rearrange("p e b -> p (e b)") for t in (fl, ps_, pt))
            then_wait(ve.tensor_tensor(fl[:, :, :], cnt[:, :].rearrange("p (e o) -> p e o", o=1).to_broadcast(levels),
                                       cc[:, C_LEVEL:C_LEVEL + EXPERTS * MORE].rearrange("p (e b) -> p e b", b=MORE),
                                       ALU.is_gt))
            then_wait(ve.memset(pt_, 1.0))
            then_wait(ve.tensor_tensor_scan(po_, pt_, fl_, 0.0, ALU.mult, ALU.add))
            then_wait(ve.tensor_scalar(code[:, 2:3], po_[:, EXPERTS * MORE - 1:EXPERTS * MORE], float(EXPERTS), None, ALU.add))
            then_wait(ve.tensor_scalar(po_, po_, cc[:, C_PIDX:C_PIDX + 1], None, ALU.is_equal))
            then_wait(ve.tensor_tensor(fl_, fl_, po_, ALU.mult))
            for n, c in ((0, C_ECODE), (1, C_BCODE)):
                then_wait(ve.tensor_tensor(pt_, fl_, cc[:, c:c + EXPERTS * MORE], ALU.mult))
                then_wait(ve.tensor_reduce(code[:, n:n + 1], pt_, AX.X, ALU.add))
            ve.tensor_copy(code[:, 2:3], code[:, 2:3]).then_inc(s_code, 1)
            slot_values(0)
            ve.wait_ge(s_row, 1)
            ve.wait_ge(s_tab0, 16)
            ve.tensor_copy(table[0:1, :, EXPERTS:EXPERTS + OVER],
                           rank_bank[0:1, 0:2 * P].rearrange("p (n o) -> p n o", n=2)[:, :, 0:OVER]).then_inc(s_tab, 1)
            ve.tensor_copy(table[0:1, 0, TABLE - 1:TABLE], code[0:1, 2:3]).then_inc(s_tab, 1)
            for unit in range(LO_AHEAD):
                lo_part(ve, 0, unit)
            for q in range(4):
                x_lo_part(0, q)
            ve.wait_ge(s_tab, 2)
            jobs = ve.value_load(table[0:1, 0, TABLE - 1:TABLE], min_val=EXPERTS, max_val=JOBS)
            with ve.Fori(0, jobs) as j:
                def lo_next(u):
                    job, unit = of(j, u + LO_AHEAD)
                    if unit not in POOL_LO:
                        lo_part(ve, job, unit)

                def whole(u, to):
                    ve.wait_ge(s_half, tile_n(j, u, 1))
                    ve.tensor_tensor(to, unit_banks[u % 2][:, :, 0:SLOTS], half[:, u % 2], ALU.add).then_inc(s_out_of, 1)

                ve.wait_ge(s_bias, j * 16 + 16)
                ve.tensor_copy(bias_cur[:, 0:KD], bias_next[:, 0:KD]).then_inc(s_bcur, 1)
                ve.tensor_copy(bias_cur[:, 2 * KD:3 * KD], bias_next[:, 2 * KD:3 * KD]).then_inc(s_bcur, 1)
                ve.tensor_scalar(bias_cur[:, KD:2 * KD], bias_next[:, KD:2 * KD], 1.0, None, ALU.add).then_inc(s_bcur, 1)
                for u in range(UNITS):
                    lo_next(u)
                    if u == 1:
                        hot(j + 1)
                    if u == 3:
                        slot_values(j + 1)
                    if u == GU:
                        x_lo_part(j + 1, 0)
                        x_lo_part(j + 1, 1)
                    if u < GU:
                        g, v = inner[:, u % 2, 0], inner[:, u % 2, 1]
                        whole(u, inner[:, u % 2])
                        ve.wait_ge(s_out_of, out_of(j, u))
                        ve.tensor_scalar(g, g, LIMIT, None, ALU.min).then_inc(s_in, 1)
                        ve.tensor_scalar(v, v, 1.0 + LIMIT, 1.0 - LIMIT, ALU.min, ALU.max).then_inc(s_in, 1)
                        ve.wait_ge(s_in, j * 2 * GU + 2 * u + 2)
                        ve.tensor_tensor(up_gate[:, u % 2], v, g, ALU.mult).then_inc(s_ug, 1)
                        ve.wait_ge(s_sig, j * GU + u + 1)
                        ve.wait_ge(s_ug, j * GU + u + 1)
                        ve.tensor_tensor(act[:, u], up_gate[:, u % 2], sig[:, u % 2], ALU.mult).then_inc(s_act, 1)
                    else:
                        i = u - GU
                        if i >= 2:
                            ve.wait_ge(s_ytr, j * 4 + i - 1)
                        whole(u, y_cols[:, i % 2, :, 0:SLOTS])
                    if u == GU:
                        x_lo_part(j + 1, 2)
                        x_lo_part(j + 1, 3)
            ve.wait_ge(s_gb2, 64)
            for i in range(NT + 1):
                if i < NT:
                    ve.wait_ge(s_fin[i], 16)
                    norm_stats(NT + i, [fin[:, i, 0:512], fin[:, i, 512:1024]])
                if i > 0:
                    norm_scale(NT + i - 1)
                    ve.wait_ge(s_xn, NT + i)
                    ve.tensor_tensor(fin[:, i - 1], fin[:, i - 1], gb2[:, 0], ALU.mult).then_inc(s_gx, 1)

        @block.gpsimd
        def _(po):
            po.wait_ge(s_zero, 1)
            for part, m in ((0, P), (1, TAIL)):
                po.dma_start(sum_rows[SEQ + part * P:SEQ + part * P + m, :], x_rows[0:m, 1]).then_inc(s_sum[part], 16)
            po.wait_ge(s_gb, 32)
            for i in range(NT):
                po.wait_ge(s_gx, i + 1)
                po.tensor_tensor(x1_t[:, i % 2], x1_t[:, i % 2], gb1[:, 1], ALU.add).then_inc(s_x1, 1)
            po.wait_ge(s_kc, 32)
            po.wait_ge(s_zero, 6)

            def columns(job, e, b):
                if not (isinstance(job, int) and job == 0):
                    po.wait_ge(s_disp, job)
                    apart(po)
                po.tensor_copy(slot_src[:, :, 3:6], gate3[:, :, bass.ds(e, 1), :].rearrange("p i o n -> p i (o n)"))\
                  .then_inc(s_pool, 1)
                po.wait_ge(s_pool, pool_n(job, 1))
                po.tensor_tensor(rank_col[:, :].rearrange("p (i o) -> p i o", o=1), rank[:, :, bass.ds(e, 1)],
                                 kc[:, bass.ds(K_BOFF + b, 1)].rearrange("p (a o) -> p a o", o=1).to_broadcast((P, NT, 1)),
                                 ALU.subtract).then_inc(s_col, 1)

            def rows(job):
                n = [1]

                def step(ins):
                    n[0] += 1
                    ins.then_inc(s_pool, 1)
                    po.wait_ge(s_pool, pool_n(job, n[0]))
                    apart(po)

                if not isinstance(job, int):
                    for s in s_sum:
                        po.wait_ge(s, job * 16)
                    apart(po)
                step(po.tensor_copy(idx_cur[:, :], idx_next[:, :]))
                step(po.tensor_copy(gate_cur[:, :], gate_next[:, :]))
                po.wait_ge(s_val, job + 1)
                v = lambda c: slot_val[:, :, c:c + 1].rearrange("p c o -> p (c o)")
                junk = kc[:, K_JUNK:K_JUNK + 2]
                step(po.tensor_tensor(tiny[:, 0], v(2), junk, ALU.mult))
                step(po.tensor_tensor(tiny[:, 0], junk, tiny[:, 0], ALU.subtract))
                step(po.tensor_tensor(tiny[:, 1], v(0), v(1), ALU.add))
                step(po.tensor_tensor(tiny[:, 1], tiny[:, 0], tiny[:, 1], ALU.add))
                step(po.tensor_tensor(tiny[:, 2], v(3), v(4), ALU.add))
                step(po.tensor_tensor(gate_next[:, :], tiny[:, 2], v(5), ALU.add))
                step(po.tensor_copy(idx_next[:, :], tiny[:, 1]))
                assert n[0] == POOL_STEPS
                wait(po, s_xtr, job * 4)
                apart(po)
                for part, m in ((0, P), (1, TAIL)):
                    po.indirect_dma_start(out=x_rows[0:m, part], out_offset=None, in_=x1_rows[:, :],
                                          in_offset=bass.IndirectOffsetOnAxis(ap=idx_next[0:m, part:part + 1], axis=0))\
                      .then_inc(s_gat[part], 16)

            po.memset(idx_next[:, :], 0).then_inc(s_init, 1)
            po.memset(gate_next[:, :], 0.0).then_inc(s_init, 1)
            po.wait_ge(s_init, 2)
            po.wait_ge(s_route, 1)
            columns(0, 0, 0)
            for s in s_st:
                po.wait_ge(s, NT // 2 * 32)
            for s in s_sum:
                po.wait_ge(s, 16)
            po.wait_ge(s_gb2, 32)
            rows(0)
            po.wait_ge(s_tab, 2)
            jobs = po.value_load(table[0:1, 0, TABLE - 1:TABLE], min_val=EXPERTS, max_val=JOBS)
            with po.Fori(0, jobs) as j:
                e = po.value_load(table[0:1, 0, bass.ds(j + 1, 1)], min_val=0, max_val=EXPERTS - 1)
                b = po.value_load(table[0:1, 1, bass.ds(j + 1, 1)], min_val=0, max_val=MORE)
                columns(j + 1, e, b)
                def act_lo(u):
                    po.wait_ge(s_ahi, j * GU + u + 1)
                    po.tensor_tensor(act_parts[:, u, 1], act[:, u], act_parts[:, u, 0].bitcast(F32), ALU.subtract)\
                      .then_inc(s_alo, 1)

                for u in range(UNITS):
                    if u == 3:
                        rows(j + 1)
                    job, unit = of(j, u + LO_AHEAD)
                    if unit in POOL_LO:
                        po.wait_ge(s_tile, tile_n(j, u - 1, -1))
                        lo_part(po, job, unit)
                    if 0 < u <= GU:
                        act_lo(u - 1)
                po.wait_ge(s_yrow, j * 4 + 5)
                for part in range(2):
                    po.wait_ge(s_sum[part], j * 16 + 16)
                apart(po)
                for part, m in ((0, P), (1, TAIL)):
                    po.indirect_dma_start(out=sum_rows[:, :],
                                          out_offset=bass.IndirectOffsetOnAxis(ap=idx_cur[0:m, part:part + 1], axis=0),
                                          in_=y_rows[0:m, part], in_offset=None, compute_op=ALU.add)\
                      .then_inc(s_sum[part], 16)
            po.wait_ge(s_gb2, 64)
            for i in range(NT):
                po.wait_ge(s_gx, NT + i + 1)
                po.tensor_tensor(fin[:, i], fin[:, i], gb2[:, 1], ALU.add).then_inc(s_x1, 1)


def constants():
    import numpy as np

    f = np.float32
    t = np.arange(P)
    row, col = t[:, None], t[None, :]
    parts = []
    for first in (False, True):
        for w in WINDOWS:
            n = np.minimum(col + 1, w) if first else np.full((1, P), w)
            parts.append(((row <= col) & (row > col - w)) / n - (row == col))
    for w in WINDOWS:
        parts.append((row - P > col[:, :REACH] - w) / f(w))
    parts.append(row < col)
    parts.append(np.tile((np.arange(NT * EXPERTS) % EXPERTS != 0)[None], (P, 1)))
    e, b = np.divmod(np.arange(EXPERTS * MORE), MORE)
    parts += [np.tile(v[None], (P, 1)) for v in (SLOTS * (b + 1), e, b + 1)]
    parts.append(row + 1)
    for i in range(NT):
        parts.append(np.concatenate([row, np.full((P, 1), i * P), np.ones((P, 1))], 1))
    consts = np.concatenate([p.astype(f) for p in parts], 1)
    assert consts.shape == (P, C_END)
    keep = np.concatenate([
        np.eye(P), np.tile(np.arange(SLOTS)[None], (P, 1)), SEQ + row, SEQ + P + row,
        np.tile(SLOTS * np.arange(MORE + 1)[None], (P, 1))], 1).astype(f)
    assert keep.shape == (P, K_END)
    table = np.zeros((1, 2, TABLE), np.int32)
    table[0, 0, :EXPERTS] = np.arange(EXPERTS)
    return np.ascontiguousarray(consts), np.ascontiguousarray(keep), table


def kernel(x, pool_w, pool_scale, sc_w_in, sc_conv_w, sc_w_out, cf_w_in, cf_b_in, cf_dw_w, cf_dw_b, cf_ln_g,
           cf_ln_b, cf_w_out, cf_b_out, mix_ln_g, mix_ln_b, router_w, router_b, moe_w_gu, moe_b_gu, moe_w_dn,
           moe_b_dn, ffn_ln_g, ffn_ln_b):
    import numpy as np
    import concourse.bacc as bacc
    from concourse.bass_utils import run_bass_kernel_spmd

    consts, keep, table = constants()
    b_gu = np.asarray(moe_b_gu)[0].reshape(EXPERTS, KD, P, 2).transpose(0, 2, 3, 1).reshape(EXPERTS, P, 2 * KD)
    b_dn = np.asarray(moe_b_dn)[0].reshape(EXPERTS, KD, P).transpose(0, 2, 1)
    arrays = {
        "x": np.asarray(x)[0],
        "w_mix": np.asarray(pool_w)[0].reshape(D, 256),
        "mix_scale": np.asarray(pool_scale),
        "ln1": np.concatenate([np.asarray(mix_ln_g), np.asarray(mix_ln_b)]),
        "ln2": np.concatenate([np.asarray(ffn_ln_g), np.asarray(ffn_ln_b)]),
        "router_w": np.asarray(router_w)[0],
        "router_b": np.asarray(router_b),
        "w_gu": np.asarray(moe_w_gu)[0],
        "w_dn": np.asarray(moe_w_dn)[0],
        "biases": np.concatenate([b_gu, b_dn], 2),
        "keep": keep,
        "consts": consts,
        "table0": table,
    }
    arrays = {n: np.ascontiguousarray(a) for n, a in arrays.items()}
    nc = bacc.Bacc("TRN2", target_bir_lowering=False, num_devices=1)
    args = [nc.dram_tensor(n, a.shape, mybir.dt.from_np(a.dtype), kind="ExternalInput").ap()
            for n, a in arrays.items()]
    out = nc.dram_tensor("out", (SEQ, D), F32, kind="ExternalOutput").ap()
    build_program(nc, *args, out)
    r = run_bass_kernel_spmd(nc, [arrays], core_ids=[0])
    return np.asarray(r.results[0]["out"]).reshape(1, SEQ, D)
```

```python
import concourse.bass as bass
from concourse import mybir
from contextlib import ExitStack

F32 = mybir.dt.float32
F32R = mybir.dt.float32r
BF16 = mybir.dt.bfloat16
I32 = mybir.dt.int32
ALU = mybir.AluOpType
ACT = mybir.ActivationFunctionType
AX = mybir.AxisListType

P = 128
D = 1024
SEQ = 1024
KD = D // P
NT = SEQ // P
GROUPS = 4
WINDOWS = (2, 4, 8, 16)
REACH = 16
HALO = (NT - 1) * REACH
EXPERTS = 32
TOPK = 4
SLOTS = 154
TAIL = SLOTS - P
QUARTERS = 4
QW = D // QUARTERS
QP = QUARTERS * TAIL
MORE = -(-SEQ // SLOTS) - 1
OVER = TOPK * SEQ // SLOTS
JOBS = EXPERTS + OVER
TABLE = 64
ALPHA = 2.0 ** 0.25
EPS = 1e-5
LIMIT = 7.0
SWIGLU = 1.702
FAR = 4096.0

GU = 8
DN = 4
UNITS = GU + DN
COLS = 256
LOADS = UNITS // 2
RAWS = 3
RING = 4
TILES = 2 * UNITS
HI_AHEAD, LO_AHEAD = 3, 2
POOL_LO = (4, 10)

POOL_STEPS = 12

K_IDENT, K_IOTA, K_JUNK, K_SCALE, K_QUARTER, K_BOFF = (
    0, P, 2 * P + QP, 2 * P + QP + 2, 2 * P + QP + 4, 2 * P + QP + 6)
K_END = K_BOFF + MORE + 1
C_BAND, C_FIRST, C_TRI = 0, GROUPS * P, 2 * GROUPS * P
C_SEG = C_TRI + P
C_LEVEL = C_SEG + NT * EXPERTS
C_ECODE = C_LEVEL + EXPERTS * MORE
C_BCODE = C_ECODE + EXPERTS * MORE
C_PIDX = C_BCODE + EXPERTS * MORE
C_TOK = C_PIDX + 1
C_END = C_TOK + 3 * NT


def pool_n(job, n):
    return job * POOL_STEPS + n


def lo_count(pool, job, unit):
    own = [u for u in range(UNITS) if (u in POOL_LO) == pool]
    return job * len(own) + len([u for u in own if u <= unit])


def build_program(nc, x, w_mix, mix_scale, ln1, ln2, router_w, router_b, w_gu, w_dn, biases, keep, consts,
                  halo, table0, out):
    x1_rows = nc.dram_tensor("x1_rows", [SEQ + SLOTS, D], F32).ap()
    sum_rows = nc.dram_tensor("sum_rows", [SEQ + SLOTS, D], F32).ap()

    x1_quarters, sum_quarters = (t.rearrange("r (q n) -> (r q) n", n=QW) for t in (x1_rows, sum_rows))

    ctx = ExitStack()
    with ctx:
        def sb(name, shape, dt=F32):
            return ctx.enter_context(nc.sbuf_tensor(name, shape, dt))

        def sem(name):
            return ctx.enter_context(nc.semaphore(name))

        region = 2 * RING * KD * COLS * 4
        sb("region", [P, region // 4])
        region_at = nc.sbuf_base - region

        raw = sb("raw", [P, RAWS, KD, 2 * COLS])
        x_rows = sb("x_rows", [P, 2, D])
        x_parts = sb("x_parts", [P, KD, 2, SLOTS], F32R)
        act = sb("act", [P, KD, SLOTS])
        act_parts = sb("act_parts", [P, KD, 2, SLOTS], F32R)
        half = sb("half", [P, 2, 2, SLOTS])
        inner = sb("inner", [P, 2, 2, SLOTS])
        sig = sb("sig", [P, 2, SLOTS])
        up_gate = sb("up_gate", [P, 2, SLOTS])
        y_cols = sb("y_cols", [P, 2, 2, P])
        y_tail = sb("y_tail", [P, 2, DN, TAIL])
        y_rows = sb("y_rows", [P, 2, D])
        onehot = sb("onehot", [P, NT, P + QP], BF16)
        slot_src = sb("slot_src", [P, NT, 6], BF16)
        slot_val = sb("slot_val", [P, 2, 6])
        rank_col = sb("rank_col", [P, NT])
        tiny = sb("tiny", [P, 5, 2])
        idx_next = sb("idx_next", [P, 2], I32)
        idx_cur = sb("idx_cur", [P, 2], I32)
        gate_next = sb("gate_next", [P, 2])
        gate_cur = sb("gate_cur", [P, 2])
        bias_next = sb("bias_next", [P, 3 * KD])
        bias_cur = sb("bias_cur", [P, 3 * KD])
        rank = sb("rank", [P, NT, EXPERTS])
        gate3 = sb("gate3", [P, NT, EXPERTS, 3], BF16)
        kc = sb("kc", [P, K_END])
        table = sb("table", [1, 2, TABLE], I32)
        ident = kc[:, K_IDENT:K_IDENT + P]

        cc = sb("cc", [P, C_END])
        x1_t = sb("x1_t", [P, 2, D])
        gb1 = sb("gb1", [P, 2, D])
        rw = sb("rw", [P, KD, EXPERTS])
        rb = sb("rb", [P, EXPERTS])
        tri = sb("tri", [P, 2, P], BF16)
        halo_x = y_rows[0:HALO, 0]
        halo_band = y_rows[0:HALO, 1, 0:GROUPS * HALO].rearrange("p (g n) -> p g n", n=HALO)
        halo_diff = x_rows[:, 0, 0:KD * HALO].rearrange("p (k n) -> p k n", n=HALO)
        mv = sb("mv", [P, 3, 18])
        sum_t = y_rows

        def place(name, shape, dt, offset):
            size = 4
            for n in shape[1:]:
                size *= n
            assert offset + size <= region
            return nc.alloc_sbuf_tensor_at(name, shape, dt, offset=region_at + offset)

        w_hi = place("w_hi", [P, RING, KD, 2, P], F32R, 0)
        w_lo = place("w_lo", [P, RING, KD, 2, P], F32R, region // 2)
        kb = 1024
        x_t = place("x_t", [P, NT, D], F32, 0)
        wm = place("wm", [P, KD, 2 * P], F32, 32 * kb)
        diffs = [place("diff", [P, KD, P], F32, 40 * kb), act[:, :, 0:P]]
        res = place("res", [P, 2, D], F32, 44 * kb)
        x1_cols = place("x1_cols", [P, KD, P], F32, 52 * kb)
        scale_b = place("scale_b", [P, D], F32, 56 * kb)
        fin = place("fin", [P, NT, D], F32, 0)
        gb2 = place("gb2", [P, 2, D], F32, 32 * kb)

        lg, big, eq, cs, sel, ex = (place(n, [P, NT, EXPERTS], F32, (56 + i) * kb)
                                    for i, n in enumerate(("lg", "big", "eq", "cs", "sel", "ex")))
        lgt = place("lgt", [EXPERTS, P], F32, 62 * kb)
        top = sb("top", [P, NT, 8])
        per = sb("per", [P, 4, NT])
        mask = sb("mask", [P, NT, EXPERTS], BF16)
        cnt = sb("cnt", [P, EXPERTS])
        fl = sb("fl", [P, EXPERTS, MORE])
        ps_ = sb("ps_", [P, EXPERTS, MORE])
        pt = sb("pt", [P, EXPERTS, MORE])
        code = sb("code", [P, 3])

        pair = [ctx.enter_context(nc.psum_tensor(f"pair{i}", [P, 2, 512], F32)) for i in range(4)]
        bank = [p[:, i] for p in pair for i in range(2)]
        unit_banks, ub, tb, dispatch_bank, rank_bank = pair[0:2], bank[0:4], bank[4:6], bank[6], bank[7]
        tail_bank = rank_bank

        s_band, s_kc, s_wm, s_gb, s_rw = sem("s_band"), sem("s_kc"), sem("s_wm"), sem("s_gb"), sem("s_rw")
        s_halo_in = sem("s_halo_in")
        s_halo, s_haloc = sem("s_halo"), sem("s_haloc")
        s_x = [sem(f"s_x_tile{i}") for i in range(NT)]
        s_scaled = sem("s_scaled")
        s_diff = sem("s_diff")
        s_diffc = sem("s_diffc")
        s_h = sem("s_h")
        s_res = sem("s_res")
        s_dve = sem("s_dve")
        s_var = sem("s_var")
        s_std = sem("s_std")
        s_nrm = sem("s_nrm")
        s_xn = sem("s_xn")
        s_gx = sem("s_gx")
        s_x1 = sem("s_x1")
        s_ax = sem("s_ax")
        s_st = [sem(f"s_st{i}") for i in range(2)]
        s_tr = sem("s_tr")
        s_trc = [sem("s_trc_act"), sem("s_trc_dve")]
        s_lg = sem("s_lg")
        s_lgc = sem("s_lgc")
        s_back = sem("s_back")
        s_ex = sem("s_ex")
        s_mask = sem("s_mask")
        s_rank = sem("s_rank")
        s_route = sem("s_route")
        s_code = sem("s_code")
        s_row = sem("s_row")
        s_tab0, s_tab = sem("s_tab0"), sem("s_tab")
        s_zero = sem("s_zero")
        s_apart = sem("s_apart")
        s_init = sem("s_init")

        s_raw = [sem(f"s_raw{i}") for i in range(RAWS)]
        s_hi = sem("s_hi")
        s_lo = [sem("s_lo_dve"), sem("s_lo_pool")]
        s_tile = sem("s_tile")
        s_half = sem("s_half")
        s_out_of = sem("s_out_of")
        s_in = sem("s_in")
        s_ug = sem("s_ug")
        s_sig = sem("s_sig")
        s_act = sem("s_act")
        s_ahi, s_alo = sem("s_ahi"), sem("s_alo")
        s_ytr = sem("s_ytr")
        s_yrow = sem("s_yrow")
        s_col = sem("s_col")
        s_hot = sem("s_hot")
        s_disp = sem("s_disp")
        s_val = sem("s_val")
        s_pool = sem("s_pool")
        s_gat = [sem("s_gat_main"), sem("s_gat_tail")]
        s_xtr = sem("s_xtr")
        s_xhi, s_xlo = sem("s_xhi"), sem("s_xlo")
        s_bias, s_bcur = sem("s_bias"), sem("s_bcur")
        s_sum = [sem("s_sum_main"), sem("s_sum_tail")]
        s_fin = [sem(f"s_fin{i}") for i in range(NT)]
        s_gb2, s_out = sem("s_gb2"), sem("s_out")

        block = ctx.enter_context(nc.Block())

        def wait(eng, s, value):
            if not isinstance(value, int) or value > 0:
                eng.wait_ge(s, value)

        def apart(eng):
            eng.sem_inc(s_apart, 1)

        def of(job, unit):
            return (job + 1, unit - UNITS) if unit >= UNITS else (job, unit)

        def tile_n(j, u, t):
            return j * TILES + 2 * u + t + 1

        def out_of(j, u):
            return j * UNITS + 2 + u + 1

        def added(j):
            return j * 16 + 32

        def y_turned(j, i):
            return j * 4 + i + 2

        def rows_out(j):
            return j * 3 + 2

        def x_piece(part, piece):
            if piece == 0:
                return x_parts[:, :, part, P:SLOTS].rearrange("p (q h) s -> p h q s", h=2)
            return x_parts[:, 4 * piece - 4:4 * piece, part, 0:P]

        def turned(piece):
            if piece == 0:
                return tail_bank[:, 0:2 * QP].rearrange("p (h q s) -> p h q s", h=2, q=QUARTERS)
            return tb[piece - 1].rearrange("p (k s) -> p k s", k=4)

        def wait_raw(eng, job, unit):
            load = unit // 2
            eng.wait_ge(s_raw[load % RAWS], (job * (LOADS // RAWS) + load // RAWS + 1) * 16)

        def wait_lo(eng, job, unit):
            pool = unit in POOL_LO
            eng.wait_ge(s_lo[pool], lo_count(pool, job, unit))

        def unit_of_raw(t, unit):
            v = t[:, unit // 2 % RAWS, :, unit % 2 * COLS:(unit % 2 + 1) * COLS]
            if unit < GU:
                return v.rearrange("p k (n t) -> p k t n", t=2)
            return v.rearrange("p k (t n) -> p k t n", t=2)

        def lo_part(eng, job, unit):
            eng.wait_ge(s_hi, job * UNITS + unit + 1)
            r = unit % RING
            eng.tensor_tensor(w_lo[:, r], unit_of_raw(raw, unit), w_hi[:, r].bitcast(F32), ALU.subtract)\
               .then_inc(s_lo[unit in POOL_LO], 1)

        @block.sync
        def _(sp):
            def load_weights(e, load):
                slot = load % RAWS
                if load < GU // 2:
                    src = w_gu[e, :, load * 2 * COLS:(load + 1) * 2 * COLS]
                else:
                    src = w_dn[e, :, (load - GU // 2) * 2 * COLS:(load - GU // 2 + 1) * 2 * COLS]
                sp.dma_start(raw[:, slot], src.rearrange("(k p) n -> p k n", p=P)).then_inc(s_raw[slot], 16)

            sp.dma_start(x_t[:, 0], x[0:P, :]).then_inc(s_x[0], 16)
            sp.dma_start(cc[:, 0:C_TRI], consts[:, 0:C_TRI]).then_inc(s_band, 16)
            sp.dma_start(wm[:, :, :], w_mix.rearrange("(k p) n -> p k n", p=P)).then_inc(s_wm, 16)
            sp.dma_start(scale_b[:, :], mix_scale.to_broadcast((P, D))).then_inc(s_wm, 16)
            sp.dma_start(halo_band, halo.rearrange("p (g n) -> p g n", n=HALO)).then_inc(s_halo_in, 16)
            for i in range(NT - 1):
                sp.dma_start(halo_x[i * REACH:(i + 1) * REACH, :], x[(i + 1) * P - REACH:(i + 1) * P, :])\
                  .then_inc(s_halo_in, 16)
            sp.dma_start(x_t[:, 1], x[P:2 * P, :]).then_inc(s_x[1], 16)
            sp.dma_start(kc[:, :], keep).then_inc(s_kc, 16)
            sp.dma_start(x_t[:, 2], x[2 * P:3 * P, :]).then_inc(s_x[2], 16)
            sp.dma_start(cc[:, C_TRI:C_END], consts[:, C_TRI:C_END]).then_inc(s_kc, 16)
            for i in range(2):
                sp.dma_start(gb1[:, i], ln1[i:i + 1, :].to_broadcast((P, D))).then_inc(s_gb, 16)
            sp.dma_start(rw[:, :, :], router_w.rearrange("(k p) n -> p k n", p=P)).then_inc(s_rw, 16)
            sp.dma_start(rb[:, :], router_b.to_broadcast((P, EXPERTS))).then_inc(s_rw, 16)
            sp.dma_start(table[:, :, :], table0).then_inc(s_tab0, 16)
            for i in range(3, NT):
                sp.dma_start(x_t[:, i], x[i * P:(i + 1) * P, :]).then_inc(s_x[i], 16)
            sp.wait_ge(s_zero, 1)
            zeros = x_rows[:, 1]
            sp.dma_start(x1_rows[SEQ:SEQ + P, :], zeros).then_inc(s_gb2, 16)
            sp.dma_start(x1_rows[SEQ + P:SEQ + SLOTS, :], zeros[0:TAIL]).then_inc(s_gb2, 16)
            for load in range(RAWS):
                load_weights(0, load)
            sp.dma_start(bias_next[:, :], biases[0]).then_inc(s_bias, 16)
            for i in range(NT):
                sp.wait_ge(s_x1, i + 1)
                sp.dma_start(x1_rows[i * P:(i + 1) * P, :], x1_t[:, i % 2]).then_inc(s_st[i % 2], 16)
                sp.wait_ge(s_ax, i + 1)
                sp.dma_start(sum_rows[i * P:(i + 1) * P, :], sum_t[:, i % 2]).then_inc(s_st[i % 2], 16)
            sp.wait_ge(s_tab, 2)
            jobs = sp.value_load(table[0:1, 0, TABLE - 1:TABLE], min_val=EXPERTS, max_val=JOBS)
            with sp.Fori(0, jobs) as j:
                for q in range(LOADS):
                    if q % RAWS == 0:
                        nxt = q // RAWS
                        e = sp.value_load(table[0:1, 0, bass.ds(j + nxt, 1)], min_val=0, max_val=EXPERTS - 1)
                    for unit in (2 * q, 2 * q + 1):
                        wait_lo(sp, j, unit)
                        apart(sp)
                    load_weights(e, (q + RAWS) % LOADS)
                    if q == RAWS:
                        sp.wait_ge(s_bcur, j * 3 + 3)
                        apart(sp)
                        sp.dma_start(bias_next[:, :], biases[e]).then_inc(s_bias, 16)
            for s in s_sum:
                sp.wait_ge(s, added(jobs))
                apart(sp)
            sp.wait_ge(s_hi, jobs * UNITS + HI_AHEAD)
            apart(sp)
            sp.wait_ge(s_lo[0], lo_count(False, jobs, LO_AHEAD - 1))
            apart(sp)
            sp.wait_ge(s_tile, jobs * TILES)
            apart(sp)
            for i in range(NT):
                sp.dma_start(fin[:, i], sum_rows[i * P:(i + 1) * P, :]).then_inc(s_fin[i], 16)
                if i < 2:
                    sp.dma_start(gb2[:, i], ln2[i:i + 1, :].to_broadcast((P, D))).then_inc(s_gb2, 16)
            for i in range(NT):
                sp.wait_ge(s_x1, NT + i + 1)
                sp.dma_start(out[i * P:(i + 1) * P, :], fin[:, i]).then_inc(s_out, 16)
            sp.wait_ge(s_out, 16 * NT)
            for i in range(RAWS):
                sp.wait_ge(s_raw[i], jobs * (LOADS // RAWS) * 16 + 16)
            apart(sp)
            sp.wait_ge(s_bias, jobs * 16 + 16)
            apart(sp)

        @block.tensor
        def _(pe):
            def windows(i):
                pe.wait_ge(s_x[i], 16)
                for half in range(2):
                    if i > 0:
                        pe.wait_ge(s_diffc, 2 * i - 1 + half)
                    for c in range(4 * half, 4 * half + 4):
                        b = (C_FIRST if i == 0 else C_BAND) + c // 2 * P
                        last = pe.matmul(ub[half][:, c % 4 * P:(c % 4 + 1) * P], x_t[:, i, c * P:(c + 1) * P],
                                         cc[:, b:b + P], start=c % 4 == 0, stop=i == 0 and c % 4 == 3,
                                         skip_group_check=True)
                    if i > 0:
                        last = pe.matmul(ub[half].rearrange("p (c n) -> p c n", n=P)[:, :, 0:REACH], ident,
                                         halo_diff[:, 4 * half:4 * half + 4, (i - 1) * REACH:i * REACH],
                                         start=False, stop=True, skip_group_check=True)
                    last.then_inc(s_diff, 1)

            def halo_windows():
                pe.wait_ge(s_halo_in, NT * 16)
                for c in range(KD):
                    last = pe.matmul(tb[c // 4][:, c % 4 * HALO:(c % 4 + 1) * HALO], halo_x[:, c * P:(c + 1) * P],
                                     halo_band[:, c // 2], start=True, stop=True)
                last.then_inc(s_halo, 1)

            def mix(i):
                for half in range(2):
                    pe.wait_ge(s_diffc, 2 * i + half + 1)
                    if i > 0:
                        pe.wait_ge(s_res, 2 * i - 1 + half)
                    for g in (2 * half, 2 * half + 1):
                        for k in range(2):
                            last = pe.matmul(ub[2 + half][:, g % 2 * 256:(g % 2 + 1) * 256],
                                             diffs[i % 2][:, 2 * g + k], wm[:, 2 * g + k], start=k == 0, stop=k == 1)
                    last.then_inc(s_h, 1)

            def turn_x1(i):
                pe.wait_ge(s_x1, i + 1)
                for half in range(2):
                    if i > 0:
                        pe.wait_ge(s_trc[half], i)
                    for c in range(4):
                        k = 4 * half + c
                        last = pe.transpose(tb[half][:, c * P:(c + 1) * P], x1_t[:, i % 2, k * P:(k + 1) * P], ident)
                    last.then_inc(s_tr, 1)

            def logits(i):
                if i > 0:
                    pe.wait_ge(s_lgc, i)
                for k in range(KD):
                    if k % 4 == 0:
                        pe.wait_ge(s_trc[k // 4], i + 1)
                    last = pe.matmul(rank_bank[0:EXPERTS, 0:P], rw[:, k], x1_cols[:, k],
                                     start=k == 0, stop=k == KD - 1)
                last.then_inc(s_lg, 1)

            def turn_logits(i):
                pe.wait_ge(s_lgc, i + 1)
                pe.transpose(dispatch_bank[:, i * EXPERTS:(i + 1) * EXPERTS], lgt[:, :], ident[0:EXPERTS, 0:EXPERTS])\
                  .then_inc(s_back, 1)

            pe.wait_ge(s_band, 16)
            windows(0)
            pe.wait_ge(s_scaled, 1)
            mix(0)
            halo_windows()
            pe.wait_ge(s_kc, 32)
            pe.wait_ge(s_haloc, 1)
            windows(1)
            for i in range(1, NT + 3):
                if i + 1 < NT:
                    windows(i + 1)
                if 2 <= i < NT + 2:
                    turn_x1(i - 2)
                if i < NT:
                    mix(i)
                if i >= 3:
                    turn_logits(i - 3)
                if i == 2:
                    pe.wait_ge(s_rw, 32)
                if 2 <= i < NT + 2:
                    logits(i - 2)
            pe.wait_ge(s_zero, 6)
            pe.wait_ge(s_mask, 1)
            r = rank_bank[:, 0:NT * EXPERTS]
            pe.matmul(r, tri[:, 0], mask[:, :, :].rearrange("p a b -> p (a b)"), start=True, stop=False)
            for i in range(NT - 1):
                o = rank_bank[:, (i + 1) * EXPERTS:NT * EXPERTS]
                pe.matmul(o, tri[:, 1], mask[:, i:i + 1].to_broadcast((P, NT - 1 - i, EXPERTS)),
                          start=False, stop=i == NT - 2)
            for i in range(NT):
                last = pe.matmul(rank_bank[:, 256:256 + EXPERTS], tri[:, 1], mask[:, i], start=i == 0, stop=i == NT - 1,
                                 skip_group_check=True)
            last.then_inc(s_rank, 1)

            def dispatch(job):
                pe.wait_ge(s_hot, job + 1)
                wait(pe, s_val, job)
                for part, m in ((0, P), (1, QP)):
                    for i in range(NT):
                        last = pe.matmul(dispatch_bank[0:m, 8 * part:8 * part + 6], onehot[:, i, part * P:part * P + m],
                                         slot_src[:, i], start=i == 0, stop=i == NT - 1)
                last.then_inc(s_disp, 1)

            def turn_x(job):
                for s in s_gat:
                    pe.wait_ge(s, job * 16 + 16)
                if not isinstance(job, int):
                    pe.wait_ge(s_yrow, rows_out(job - 1))
                for h in range(2):
                    last = pe.transpose(tail_bank[:, h * QP:(h + 1) * QP], x_rows[0:QP, 1, h * P:(h + 1) * P],
                                        ident[0:QP, 0:QP])
                last.then_inc(s_xtr, 1)
                for piece in range(2):
                    for c in range(4):
                        k = 4 * piece + c
                        last = pe.transpose(tb[piece][:, c * P:(c + 1) * P], x_rows[:, 0, k * P:(k + 1) * P], ident)
                    last.then_inc(s_xtr, 1)

            def turn_y(j, i):
                pe.wait_ge(s_out_of, out_of(j, GU + i))
                if i == 0:
                    pe.wait_ge(s_xlo, j * 3 + 6)
                for t in range(2):
                    c = (2 * i + t) % 4 * P
                    last = pe.transpose(tb[i // 2][:, c:c + P], y_cols[:, i % 2, t], ident)
                if i == DN - 1:
                    for h in range(2):
                        last = pe.transpose(tail_bank[0:QP, h * P:(h + 1) * P],
                                            y_tail[:, h].rearrange("p q s -> p (q s)"), ident)
                last.then_inc(s_ytr, 1)

            def products(j, u):
                pe.wait_ge(s_hi, j * UNITS + u + 1)
                wait_lo(pe, j, u)
                parts = x_parts if u < GU else act_parts
                r = u % RING
                pe.wait_ge(s_out_of, out_of(j, u - 2))
                order = [(t, k) for t in range(2) for k in range(KD)]
                if u == GU:
                    order.sort(key=lambda tk: tk[1] == KD - 1)
                for n, (t, k) in enumerate(order):
                    o = ub[u % 2 * 2 + t]
                    if u == GU and (t, k) in ((0, 0), (0, KD - 1)):
                        chunks = j * GU + (KD - 1 if k == 0 else KD)
                        pe.wait_ge(s_ahi, chunks)
                        pe.wait_ge(s_alo, chunks)
                    if u == 0 and t == 0 and k % 4 == 0:
                        pe.wait_ge(s_xlo, j * 3 + k // 4 + 2)
                    for lo in ((0, 1) if k == 0 else (1, 0)):
                        if lo:
                            pe.matmul(o[:, SLOTS:2 * SLOTS], w_lo[:, r, k, t], parts[:, k, 0],
                                      start=False, stop=False)
                        else:
                            last = pe.matmul(o[:, 0:2 * SLOTS], w_hi[:, r, k, t],
                                             parts[:, k].rearrange("p a b -> p (a b)"),
                                             start=k == 0, stop=k == KD - 1)
                    if k == KD - 1:
                        last.then_inc(s_tile, 1)

            pe.wait_ge(s_route, 1)
            pe.wait_ge(s_res, 2 * NT)
            pe.wait_ge(s_diffc, 2 * NT)
            dispatch(0)
            pe.wait_ge(s_code, 1)
            for n in range(2):
                last = pe.matmul(rank_bank[0:1, n * P:(n + 1) * P], code[:, n:n + 1], ident, start=True, stop=True)
            last.then_inc(s_row, 1)
            pe.wait_ge(s_tab, 2)
            turn_x(0)
            jobs = pe.value_load(table[0:1, 0, TABLE - 1:TABLE], min_val=EXPERTS, max_val=JOBS)
            with pe.Fori(0, jobs) as j:
                for u in range(UNITS):
                    products(j, u)
                    if u == 0:
                        turn_y(j - 1, DN - 1)
                    if u == 3:
                        dispatch(j + 1)
                    if u == GU - 1:
                        turn_x(j + 1)
                    if u > GU:
                        turn_y(j, u - GU - 1)
            turn_y(jobs - 1, DN - 1)

        @block.scalar
        def _(ac):
            def hi_part(job, unit):
                wait_raw(ac, job, unit)
                ac.activation(w_hi[:, unit % RING], unit_of_raw(raw, unit), ACT.Copy).then_inc(s_hi, 1)

            def copy_diff(i):
                for half in range(2):
                    ac.wait_ge(s_diff, 2 * i + half + 1)
                    if i > 1:
                        ac.wait_ge(s_h, 2 * i - 3 + half)
                    ac.activation(diffs[i % 2][:, 4 * half:4 * half + 4], ub[half].rearrange("p (a b) -> p a b", b=P),
                                  ACT.Copy).then_inc(s_diffc, 1)

            def normalise(n, src):
                ac.wait_ge(s_var, n + 1)
                m = mv[:, n % 3]
                ac.activation(m[:, 15:16], m[:, 14:15], ACT.Sqrt).then_inc(s_std, 1)
                ac.wait_ge(s_nrm, n + 1)
                ac.activation(src, src, ACT.Identity, scale=m[:, 16:17], bias=m[:, 17:18]).then_inc(s_xn, 1)

            def store_sum(i):
                ac.wait_ge(s_x1, i + 1)
                if i >= 2:
                    ac.wait_ge(s_st[i % 2], i // 2 * 32)
                ac.activation(sum_t[:, i % 2], x1_t[:, i % 2], ACT.Copy, scale=ALPHA).then_inc(s_ax, 1)

            def copy_x1(i):
                ac.wait_ge(s_tr, 2 * i + 1)
                if i > 0:
                    ac.wait_ge(s_lg, i)
                ac.activation(x1_cols[:, 0:4].rearrange("p a b -> p (a b)"), tb[0], ACT.Copy)\
                  .then_inc(s_trc[0], 1)

            def copy_logits(i):
                ac.wait_ge(s_lg, i + 1)
                if i > 0:
                    ac.wait_ge(s_back, i)
                ac.activation(lgt[:, :], rank_bank[0:EXPERTS, 0:P], ACT.Copy).then_inc(s_lgc, 1)

            copy_diff(0)
            copy_diff(1)
            for i in range(1, NT + 3):
                if i >= 3:
                    copy_logits(i - 3)
                if i + 1 < NT:
                    copy_diff(i + 1)
                if i <= NT:
                    normalise(i - 1, res[:, (i - 1) % 2])
                if 2 <= i < NT + 2:
                    copy_x1(i - 2)
                    store_sum(i - 2)
                unit = i // 2 - 1
                if i % 2 == 0 and unit < HI_AHEAD:
                    ac.wait_ge(s_res, 2 * (2 * unit + 2))
                    hi_part(0, unit)
            ac.wait_ge(s_ex, 1)
            ac.activation(ex[:, :, :], ex[:, :, :], ACT.Exp).then_inc(s_ex, 1)

            def copy_x(job):
                for piece in range(3):
                    ac.wait_ge(s_xtr, job * 3 + piece + 1)
                    ac.activation(x_piece(0, piece), turned(piece), ACT.Copy).then_inc(s_xhi, 1)

            def y_out(j, half):
                ac.wait_ge(s_ytr, y_turned(j, 2 * half + 1))
                if half == 0:
                    ac.wait_ge(s_pool, pool_n(j + 1, 3))
                    for s in s_sum:
                        ac.wait_ge(s, added(j))
                ac.activation(y_rows[:, 0, half * 512:half * 512 + 512], tb[half], ACT.Copy,
                              scale=gate_cur[:, 0:1]).then_inc(s_yrow, 1)
                if half == 1:
                    ac.activation(y_rows[0:QP, 1, 0:QW], tail_bank[0:QP, 0:QW], ACT.Copy,
                                  scale=gate_cur[0:QP, 1:2]).then_inc(s_yrow, 1)

            copy_x(0)
            for s in s_st:
                ac.wait_ge(s, NT // 2 * 32)
            ac.wait_ge(s_pool, 3)
            ac.wait_ge(s_tab, 2)
            jobs = ac.value_load(table[0:1, 0, TABLE - 1:TABLE], min_val=EXPERTS, max_val=JOBS)
            with ac.Fori(0, jobs) as j:
                def split_act(u):
                    ac.wait_ge(s_act, j * GU + u + 1)
                    ac.activation(act_parts[:, u, 0], act[:, u], ACT.Copy).then_inc(s_ahi, 1)

                def second_half(u, t):
                    ac.wait_ge(s_tile, tile_n(j, u, t))
                    b = t * KD + u if u < GU else 2 * KD + 2 * (u - GU) + t
                    ac.activation(half[:, u % 2, t], ub[u % 2 * 2 + t][:, SLOTS:2 * SLOTS],
                                  ACT.Identity, bias=bias_cur[:, b:b + 1]).then_inc(s_half, 1)

                ac.activation(tiny[:, 3, 1:2], kc[:, 0:1], ACT.Sigmoid)
                ac.wait_ge(s_bcur, j * 3 + 3)
                for u in range(UNITS):
                    if u == GU:
                        copy_x(j + 1)
                    hi_part(*of(j, u + HI_AHEAD))
                    if 0 < u < GU:
                        split_act(u - 1)
                    if u == UNITS - 1:
                        y_out(j, 0)
                    second_half(u, 0)
                    second_half(u, 1)
                    if u < GU:
                        ac.wait_ge(s_in, j * 2 * GU + 2 * u + 1)
                        ac.activation(sig[:, u % 2], inner[:, u % 2, 0], ACT.Sigmoid, scale=SWIGLU).then_inc(s_sig, 1)
                    if u == 0:
                        y_out(j - 1, 1)
                    if u == GU - 1:
                        split_act(u)
            y_out(jobs - 1, 1)
            for i in range(NT):
                normalise(NT + i, fin[:, i])

        @block.vector
        def _(ve):
            done = [0]

            def then_wait(ins):
                done[0] += 1
                ins.then_inc(s_dve, 1)
                ve.wait_ge(s_dve, done[0])

            def norm_stats(n, halves):
                m = mv[:, n % 3]
                for half in range(2):
                    last = ve.bn_stats(m[:, 6 * half:6 * half + 6], halves[half])
                then_wait(last)
                then_wait(ve.bn_aggr(m[:, 12:14], m[:, 0:12]))
                ve.tensor_scalar(m[:, 14:15], m[:, 13:14], EPS, None, ALU.add).then_inc(s_var, 1)

            def norm_scale(n):
                m = mv[:, n % 3]
                ve.wait_ge(s_std, n + 1)
                then_wait(ve.reciprocal(m[:, 16:17], m[:, 15:16]))
                ve.tensor_scalar(m[:, 17:18], m[:, 12:13], m[:, 16:17], -1.0, ALU.mult, ALU.mult).then_inc(s_nrm, 1)

            ve.memset(x_rows[:, 1], 0.0).then_inc(s_zero, 1)
            ve.memset(y_cols[:, 1], 0.0).then_inc(s_zero, 1)
            ve.memset(y_tail[:, :, :, :], 0.0).then_inc(s_zero, 1)
            ve.wait_ge(s_wm, 32)
            ve.tensor_tensor(wm[:, :, :].rearrange("p (g k) n -> p g k n", k=2),
                             wm[:, :, :].rearrange("p (g k) n -> p g k n", k=2),
                             scale_b[:, :].rearrange("p (g o n) -> p g o n", g=GROUPS, o=1)
                             .to_broadcast((P, GROUPS, 2, 256)), ALU.mult).then_inc(s_scaled, 1)
            ve.wait_ge(s_halo, 1)
            for h in range(2):
                last = ve.tensor_copy(halo_diff[:, 4 * h:4 * h + 4],
                                      tb[h][:, 0:4 * HALO].rearrange("p (k n) -> p k n", n=HALO))
            last.then_inc(s_haloc, 1)

            def fixed_parts():
                ve.wait_ge(s_kc, 32)
                ve.tensor_copy(tri[:, 0], cc[:, C_TRI:C_TRI + P]).then_inc(s_zero, 1)
                ve.memset(tri[:, 1], 1.0).then_inc(s_zero, 1)
                ve.tensor_copy(slot_src[:, :, 0:3],
                               cc[:, C_TOK:C_TOK + 3 * NT].rearrange("p (i c) -> p i c", c=3)).then_inc(s_zero, 1)

            def residual(i):
                ve.wait_ge(s_x[i], 16)
                if i >= 2:
                    ve.wait_ge(s_gx, i - 1)
                for half in range(2):
                    ve.wait_ge(s_h, 2 * i + half + 1)
                    cols = slice(half * 512, half * 512 + 512)
                    ve.scalar_tensor_tensor(res[:, i % 2, cols], x_t[:, i, cols], ALPHA, ub[2 + half],
                                            ALU.mult, ALU.add).then_inc(s_res, 1)
                ve.wait_ge(s_res, 2 * i + 2)
                norm_stats(i, [res[:, i % 2, 0:512], res[:, i % 2, 512:1024]])

            def times_g(i):
                ve.wait_ge(s_xn, i + 1)
                if i >= 2:
                    ve.wait_ge(s_st[i % 2], i // 2 * 32)
                    ve.wait_ge(s_tr, 2 * i - 2)
                    ve.wait_ge(s_ax, i - 1)
                ve.tensor_tensor(x1_t[:, i % 2], res[:, i % 2], gb1[:, 0], ALU.mult).then_inc(s_gx, 1)

            def copy_x1(i):
                ve.wait_ge(s_tr, 2 * i + 2)
                if i > 0:
                    ve.wait_ge(s_lg, i)
                ve.tensor_copy(x1_cols[:, 4:8].rearrange("p a b -> p (a b)"), tb[1]).then_inc(s_trc[1], 1)

            residual(0)
            fixed_parts()
            ve.wait_ge(s_gb, 32)
            for i in range(1, NT + 2):
                if i <= NT:
                    norm_scale(i - 1)
                if i >= 2:
                    copy_x1(i - 2)
                if i <= NT:
                    times_g(i - 1)
                if i < NT:
                    residual(i)
            for unit in range(LO_AHEAD):
                lo_part(ve, 0, unit)

            ve.wait_ge(s_back, NT)
            ve.wait_ge(s_rw, 32)
            flat = dispatch_bank[:, 0:NT * EXPERTS].rearrange("p (i e) -> p i e", e=EXPERTS)
            whole = (P, NT, EXPERTS)
            then_wait(ve.tensor_tensor(lg[:, :, :], flat, rb[:, :].rearrange("p (o e) -> p o e", o=1).to_broadcast(whole),
                                       ALU.add))
            for i in range(NT):
                last = ve.max(top[:, i], lg[:, i])
            then_wait(last)
            fourth = top[:, :, TOPK - 1:TOPK].to_broadcast(whole)
            ve.tensor_tensor(ex[:, :, :], lg[:, :, :], top[:, :, 0:1].to_broadcast(whole), ALU.subtract).then_inc(s_ex, 1)
            then_wait(ve.tensor_tensor(big[:, :, :], lg[:, :, :], fourth, ALU.is_gt))
            then_wait(ve.tensor_tensor(eq[:, :, :], lg[:, :, :], fourth, ALU.is_equal))
            then_wait(ve.tensor_reduce(per[:, 0], big[:, :, :], AX.X, ALU.add))
            then_wait(ve.tensor_scalar(per[:, 1], per[:, 0], -1.0, float(TOPK), ALU.mult, ALU.add))
            line = lambda t: t[:, :, :].rearrange("p i e -> p (i e)")
            then_wait(ve.tensor_tensor_scan(line(cs), cc[:, C_SEG:C_SEG + NT * EXPERTS], line(eq), 0.0, ALU.mult, ALU.add))
            then_wait(ve.tensor_tensor(cs[:, :, :], cs[:, :, :],
                                       per[:, 1].rearrange("p (i o) -> p i o", o=1).to_broadcast(whole), ALU.is_le))
            then_wait(ve.tensor_tensor(cs[:, :, :], cs[:, :, :], eq[:, :, :], ALU.mult))
            then_wait(ve.tensor_tensor(sel[:, :, :], cs[:, :, :], big[:, :, :], ALU.add))
            ve.tensor_copy(mask[:, :, :], sel[:, :, :]).then_inc(s_mask, 1)
            ve.wait_ge(s_ex, 2)
            then_wait(ve.tensor_tensor(ex[:, :, :], ex[:, :, :], sel[:, :, :], ALU.mult))
            then_wait(ve.tensor_reduce(per[:, 2], ex[:, :, :], AX.X, ALU.add))
            then_wait(ve.reciprocal(per[:, 3], per[:, 2]))
            then_wait(ve.tensor_tensor(ex[:, :, :], ex[:, :, :],
                                       per[:, 3].rearrange("p (i o) -> p i o", o=1).to_broadcast(whole), ALU.mult))
            part = lambda n: gate3[:, :, :, n:n + 1].rearrange("p i e o -> p i (e o)")
            for n in range(2):
                then_wait(ve.tensor_copy(part(n), ex[:, :, :]))
                then_wait(ve.tensor_tensor(ex[:, :, :], ex[:, :, :], part(n), ALU.subtract))
            then_wait(ve.tensor_copy(part(2), ex[:, :, :]))
            then_wait(ve.tensor_scalar(sel[:, :, :], sel[:, :, :], -FAR, FAR, ALU.mult, ALU.add))
            ve.wait_ge(s_rank, 1)
            then_wait(ve.tensor_tensor(rank[:, :, :], sel[:, :, :],
                                       rank_bank[:, 0:NT * EXPERTS].rearrange("p (i e) -> p i e", e=EXPERTS), ALU.add))
            then_wait(ve.tensor_copy(cnt[:, :], rank_bank[:, 256:256 + EXPERTS]))
            ve.tensor_copy(per[:, 0, 0:1], rank[:, 0, 0:1]).then_inc(s_route, 1)

            def hot(job):
                ve.wait_ge(s_col, job + 1)
                if not (isinstance(job, int) and job == 0):
                    ve.wait_ge(s_disp, job)
                shape = (P, NT, P + QP)
                ve.tensor_tensor(onehot[:, :, :],
                                 rank_col[:, :].rearrange("p (i o) -> p i o", o=1).to_broadcast(shape),
                                 kc[:, K_IOTA:K_IOTA + P + QP].rearrange("p (o s) -> p o s", o=1).to_broadcast(shape),
                                 ALU.is_equal).then_inc(s_hot, 1)

            def slot_values(job):
                ve.wait_ge(s_disp, job + 1)
                if not (isinstance(job, int) and job == 0):
                    ve.wait_ge(s_pool, pool_n(job - 1, 9))
                ve.tensor_copy(slot_val[:, :, :],
                               dispatch_bank[:, 0:16].rearrange("p (c n) -> p c n", n=8)[:, :, 0:6]).then_inc(s_val, 1)

            def x_lo_part(job):
                for piece in range(3):
                    ve.wait_ge(s_xhi, job * 3 + piece + 1)
                    ve.tensor_tensor(x_piece(1, piece), turned(piece), x_piece(0, piece).bitcast(F32), ALU.subtract)\
                      .then_inc(s_xlo, 1)

            ve.tensor_copy(tiny[:, 4, 0:1], kc[:, 0:1]).then_inc(s_out_of, 2)
            hot(0)
            levels = (P, EXPERTS, MORE)
            fl_, po_, pt_ = (t[:, :, :].rearrange("p e b -> p (e b)") for t in (fl, ps_, pt))
            then_wait(ve.tensor_tensor(fl[:, :, :], cnt[:, :].rearrange("p (e o) -> p e o", o=1).to_broadcast(levels),
                                       cc[:, C_LEVEL:C_LEVEL + EXPERTS * MORE].rearrange("p (e b) -> p e b", b=MORE),
                                       ALU.is_gt))
            then_wait(ve.memset(pt_, 1.0))
            slot_values(0)
            then_wait(ve.tensor_tensor_scan(po_, pt_, fl_, 0.0, ALU.mult, ALU.add))
            then_wait(ve.tensor_scalar(code[:, 2:3], po_[:, EXPERTS * MORE - 1:EXPERTS * MORE], float(EXPERTS), None, ALU.add))
            then_wait(ve.tensor_scalar(po_, po_, cc[:, C_PIDX:C_PIDX + 1], None, ALU.is_equal))
            then_wait(ve.tensor_tensor(fl_, fl_, po_, ALU.mult))
            for n, c in ((0, C_ECODE), (1, C_BCODE)):
                then_wait(ve.tensor_tensor(pt_, fl_, cc[:, c:c + EXPERTS * MORE], ALU.mult))
                then_wait(ve.tensor_reduce(code[:, n:n + 1], pt_, AX.X, ALU.add))
            ve.tensor_copy(code[:, 2:3], code[:, 2:3]).then_inc(s_code, 1)
            ve.wait_ge(s_row, 1)
            ve.wait_ge(s_tab0, 16)
            ve.tensor_copy(table[0:1, :, EXPERTS:EXPERTS + OVER],
                           rank_bank[0:1, 0:2 * P].rearrange("p (n o) -> p n o", n=2)[:, :, 0:OVER]).then_inc(s_tab, 1)
            ve.tensor_copy(table[0:1, 0, TABLE - 1:TABLE], code[0:1, 2:3]).then_inc(s_tab, 1)
            x_lo_part(0)
            ve.wait_ge(s_tab, 2)
            jobs = ve.value_load(table[0:1, 0, TABLE - 1:TABLE], min_val=EXPERTS, max_val=JOBS)
            with ve.Fori(0, jobs) as j:
                def lo_next(u):
                    job, unit = of(j, u + LO_AHEAD)
                    if unit not in POOL_LO:
                        lo_part(ve, job, unit)

                def whole(u, *to):
                    ve.wait_ge(s_half, tile_n(j, u, 1))
                    at = 0
                    for t in to:
                        cols = slice(at, at + t.shape[-1])
                        last = ve.tensor_tensor(t, unit_banks[u % 2][:, :, cols], half[:, u % 2, :, cols], ALU.add)
                        at += t.shape[-1]
                    last.then_inc(s_out_of, 1)

                ve.wait_ge(s_bias, j * 16 + 16)
                ve.tensor_copy(bias_cur[:, 0:KD], bias_next[:, 0:KD]).then_inc(s_bcur, 1)
                ve.tensor_copy(bias_cur[:, 2 * KD:3 * KD], bias_next[:, 2 * KD:3 * KD]).then_inc(s_bcur, 1)
                ve.tensor_scalar(bias_cur[:, KD:2 * KD], bias_next[:, KD:2 * KD], 1.0, None, ALU.add).then_inc(s_bcur, 1)
                for u in range(UNITS):
                    lo_next(u)
                    if u == 2:
                        hot(j + 1)
                    if u == 3:
                        slot_values(j + 1)
                    if u == GU:
                        x_lo_part(j + 1)
                    if u < GU:
                        g, v = inner[:, u % 2, 0], inner[:, u % 2, 1]
                        whole(u, inner[:, u % 2])
                        ve.wait_ge(s_out_of, out_of(j, u))
                        ve.tensor_scalar(g, g, LIMIT, None, ALU.min).then_inc(s_in, 1)
                        ve.tensor_scalar(v, v, 1.0 + LIMIT, 1.0 - LIMIT, ALU.min, ALU.max).then_inc(s_in, 1)
                        ve.wait_ge(s_in, j * 2 * GU + 2 * u + 2)
                        ve.tensor_tensor(up_gate[:, u % 2], v, g, ALU.mult).then_inc(s_ug, 1)
                        ve.wait_ge(s_sig, j * GU + u + 1)
                        ve.wait_ge(s_ug, j * GU + u + 1)
                        ve.tensor_tensor(act[:, u], up_gate[:, u % 2], sig[:, u % 2], ALU.mult).then_inc(s_act, 1)
                    else:
                        i = u - GU
                        ve.wait_ge(s_ytr, y_turned(j, i - 2) if i >= 2 else y_turned(j - 1, DN - 1))
                        whole(u, y_cols[:, i % 2], y_tail[:, :, i])
            ve.wait_ge(s_gb2, 64)
            for i in range(NT + 2):
                if i < NT:
                    ve.wait_ge(s_fin[i], 16)
                    norm_stats(NT + i, [fin[:, i, 0:512], fin[:, i, 512:1024]])
                if 0 < i <= NT:
                    norm_scale(NT + i - 1)
                if i > 1:
                    ve.wait_ge(s_xn, NT + i - 1)
                    ve.tensor_tensor(fin[:, i - 2], fin[:, i - 2], gb2[:, 0], ALU.mult).then_inc(s_gx, 1)

        @block.gpsimd
        def _(po):
            po.wait_ge(s_zero, 1)
            for part, m in ((0, P), (1, TAIL)):
                po.dma_start(sum_rows[SEQ + part * P:SEQ + part * P + m, :], x_rows[0:m, 1]).then_inc(s_sum[part], 16)
            po.wait_ge(s_gb, 32)
            for i in range(NT):
                po.wait_ge(s_gx, i + 1)
                po.tensor_tensor(x1_t[:, i % 2], x1_t[:, i % 2], gb1[:, 1], ALU.add).then_inc(s_x1, 1)
            po.wait_ge(s_kc, 32)
            po.wait_ge(s_zero, 6)

            def columns(job, e, b):
                if not (isinstance(job, int) and job == 0):
                    po.wait_ge(s_disp, job)
                    apart(po)
                po.tensor_copy(slot_src[:, :, 3:6], gate3[:, :, bass.ds(e, 1), :].rearrange("p i o n -> p i (o n)"))\
                  .then_inc(s_pool, 1)
                po.wait_ge(s_pool, pool_n(job, 1))
                po.tensor_tensor(rank_col[:, :].rearrange("p (i o) -> p i o", o=1), rank[:, :, bass.ds(e, 1)],
                                 kc[:, bass.ds(K_BOFF + b, 1)].rearrange("p (a o) -> p a o", o=1).to_broadcast((P, NT, 1)),
                                 ALU.subtract).then_inc(s_col, 1)

            def rows(job):
                n = [1]

                def step(ins):
                    n[0] += 1
                    ins.then_inc(s_pool, 1)
                    po.wait_ge(s_pool, pool_n(job, n[0]))
                    apart(po)

                if not isinstance(job, int):
                    for s in s_sum:
                        po.wait_ge(s, added(job - 1))
                    apart(po)
                step(po.tensor_copy(idx_cur[:, :], idx_next[:, :]))
                step(po.tensor_copy(gate_cur[:, :], gate_next[:, :]))
                po.wait_ge(s_val, job + 1)
                v = lambda c: slot_val[:, :, c:c + 1].rearrange("p c o -> p (c o)")
                junk = kc[:, K_JUNK:K_JUNK + 2]
                step(po.tensor_tensor(tiny[:, 0], v(2), junk, ALU.mult))
                step(po.tensor_tensor(tiny[:, 0], junk, tiny[:, 0], ALU.subtract))
                step(po.tensor_tensor(tiny[:, 1], v(0), v(1), ALU.add))
                step(po.tensor_tensor(tiny[:, 1], tiny[:, 0], tiny[:, 1], ALU.add))
                step(po.tensor_tensor(tiny[:, 2], v(3), v(4), ALU.add))
                step(po.tensor_tensor(gate_next[:, :], tiny[:, 2], v(5), ALU.add))
                step(po.tensor_tensor(tiny[:, 1], tiny[:, 1], kc[:, K_SCALE:K_SCALE + 2], ALU.mult))
                step(po.tensor_tensor(tiny[:, 1], tiny[:, 1], kc[:, K_QUARTER:K_QUARTER + 2], ALU.add))
                step(po.tensor_copy(idx_next[:, :], tiny[:, 1]))
                assert n[0] == POOL_STEPS
                wait(po, s_xtr, job * 3)
                apart(po)
                for part, src, m, n in ((0, x1_rows, P, D), (1, x1_quarters, QP, QW)):
                    po.indirect_dma_start(out=x_rows[0:m, part, 0:n], out_offset=None, in_=src[:, :],
                                          in_offset=bass.IndirectOffsetOnAxis(ap=idx_next[0:m, part:part + 1], axis=0))\
                      .then_inc(s_gat[part], 16)

            def add_rows(j):
                po.wait_ge(s_yrow, rows_out(j))
                for part in range(2):
                    po.wait_ge(s_sum[part], j * 16 + 16)
                apart(po)
                for part, to, m, n in ((0, sum_rows, P, D), (1, sum_quarters, QP, QW)):
                    po.indirect_dma_start(out=to[:, :],
                                          out_offset=bass.IndirectOffsetOnAxis(ap=idx_cur[0:m, part:part + 1], axis=0),
                                          in_=y_rows[0:m, part, 0:n], in_offset=None, compute_op=ALU.add)\
                      .then_inc(s_sum[part], 16)

            po.tensor_tensor(tiny[:, 0], kc[:, K_JUNK:K_JUNK + 2], kc[:, K_SCALE:K_SCALE + 2], ALU.mult).then_inc(s_init, 1)
            po.wait_ge(s_init, 1)
            po.tensor_tensor(tiny[:, 0], tiny[:, 0], kc[:, K_QUARTER:K_QUARTER + 2], ALU.add).then_inc(s_init, 1)
            po.wait_ge(s_init, 2)
            po.tensor_copy(idx_next[:, :], tiny[:, 0]).then_inc(s_init, 1)
            po.memset(gate_next[:, :], 0.0).then_inc(s_init, 1)
            po.wait_ge(s_init, 4)
            po.wait_ge(s_route, 1)
            columns(0, 0, 0)
            for s in s_st:
                po.wait_ge(s, NT // 2 * 32)
            for s in s_sum:
                po.wait_ge(s, 16)
            po.wait_ge(s_gb2, 32)
            rows(0)
            po.wait_ge(s_tab, 2)
            jobs = po.value_load(table[0:1, 0, TABLE - 1:TABLE], min_val=EXPERTS, max_val=JOBS)
            with po.Fori(0, jobs) as j:
                e = po.value_load(table[0:1, 0, bass.ds(j + 1, 1)], min_val=0, max_val=EXPERTS - 1)
                b = po.value_load(table[0:1, 1, bass.ds(j + 1, 1)], min_val=0, max_val=MORE)
                columns(j + 1, e, b)
                def act_lo(u):
                    po.wait_ge(s_ahi, j * GU + u + 1)
                    po.tensor_tensor(act_parts[:, u, 1], act[:, u], act_parts[:, u, 0].bitcast(F32), ALU.subtract)\
                      .then_inc(s_alo, 1)

                for u in range(UNITS):
                    job, unit = of(j, u + LO_AHEAD)
                    if u == 4:
                        rows(j + 1)
                    if u == GU:
                        act_lo(u - 1)
                    if unit in POOL_LO:
                        po.wait_ge(s_tile, tile_n(j, u - 1, -1))
                        lo_part(po, job, unit)
                    if 0 < u < GU:
                        act_lo(u - 1)
                    if u == 1:
                        add_rows(j)
            add_rows(jobs)
            po.wait_ge(s_gb2, 64)
            for i in range(NT):
                po.wait_ge(s_gx, NT + i + 1)
                po.tensor_tensor(fin[:, i], fin[:, i], gb2[:, 1], ALU.add).then_inc(s_x1, 1)


def constants():
    import numpy as np

    f = np.float32
    t = np.arange(P)
    row, col = t[:, None], t[None, :]
    parts = []
    for first in (False, True):
        for w in WINDOWS:
            n = np.minimum(col + 1, w) if first else np.full((1, P), w)
            parts.append(((row <= col) & (row > col - w)) / n - (row == col))
    parts.append(row < col)
    parts.append(np.tile((np.arange(NT * EXPERTS) % EXPERTS != 0)[None], (P, 1)))
    e, b = np.divmod(np.arange(EXPERTS * MORE), MORE)
    parts += [np.tile(v[None], (P, 1)) for v in (SLOTS * (b + 1), e, b + 1)]
    parts.append(row + 1)
    for i in range(NT):
        parts.append(np.concatenate([row, np.full((P, 1), i * P), np.ones((P, 1))], 1))
    consts = np.concatenate([p.astype(f) for p in parts], 1)
    assert consts.shape == (P, C_END)
    r, c = np.arange(HALO)[:, None], np.arange(HALO)[None, :]
    halo = np.concatenate([(r // REACH == c // REACH) * (r % REACH - REACH > c % REACH - w) / w for w in WINDOWS],
                          1).astype(f)
    keep = np.concatenate([
        np.eye(P), np.tile(col, (P, 1)), np.tile(P + col[:, :QP] % TAIL, (P, 1)),
        SEQ + row, SEQ + P + row % TAIL, np.full((P, 1), 1), np.full((P, 1), QUARTERS), 0 * row, row // TAIL,
        np.tile(SLOTS * np.arange(MORE + 1)[None], (P, 1))], 1).astype(f)
    assert keep.shape == (P, K_END)
    table = np.zeros((1, 2, TABLE), np.int32)
    table[0, 0, :EXPERTS] = np.arange(EXPERTS)
    return np.ascontiguousarray(consts), np.ascontiguousarray(keep), halo, table


def kernel(x, pool_w, pool_scale, sc_w_in, sc_conv_w, sc_w_out, cf_w_in, cf_b_in, cf_dw_w, cf_dw_b, cf_ln_g,
           cf_ln_b, cf_w_out, cf_b_out, mix_ln_g, mix_ln_b, router_w, router_b, moe_w_gu, moe_b_gu, moe_w_dn,
           moe_b_dn, ffn_ln_g, ffn_ln_b):
    import numpy as np
    import concourse.bacc as bacc
    from concourse.bass_utils import run_bass_kernel_spmd

    consts, keep, halo, table = constants()
    b_gu = np.asarray(moe_b_gu)[0].reshape(EXPERTS, KD, P, 2).transpose(0, 2, 3, 1).reshape(EXPERTS, P, 2 * KD)
    b_dn = np.asarray(moe_b_dn)[0].reshape(EXPERTS, KD, P).transpose(0, 2, 1)
    arrays = {
        "x": np.asarray(x)[0],
        "w_mix": np.asarray(pool_w)[0].reshape(D, 256),
        "mix_scale": np.asarray(pool_scale),
        "ln1": np.concatenate([np.asarray(mix_ln_g), np.asarray(mix_ln_b)]),
        "ln2": np.concatenate([np.asarray(ffn_ln_g), np.asarray(ffn_ln_b)]),
        "router_w": np.asarray(router_w)[0],
        "router_b": np.asarray(router_b),
        "w_gu": np.asarray(moe_w_gu)[0],
        "w_dn": np.asarray(moe_w_dn)[0],
        "biases": np.concatenate([b_gu, b_dn], 2),
        "keep": keep,
        "consts": consts,
        "halo": halo,
        "table0": table,
    }
    arrays = {n: np.ascontiguousarray(a) for n, a in arrays.items()}
    nc = bacc.Bacc("TRN2", target_bir_lowering=False, num_devices=1)
    args = [nc.dram_tensor(n, a.shape, mybir.dt.from_np(a.dtype), kind="ExternalInput").ap()
            for n, a in arrays.items()]
    out = nc.dram_tensor("out", (SEQ, D), F32, kind="ExternalOutput").ap()
    build_program(nc, *args, out)
    r = run_bass_kernel_spmd(nc, [arrays], core_ids=[0])
    return np.asarray(r.results[0]["out"]).reshape(1, SEQ, D)
```

```python
import concourse.bass as bass
from concourse import mybir
from contextlib import ExitStack

F32 = mybir.dt.float32
F32R = mybir.dt.float32r
BF16 = mybir.dt.bfloat16
I32 = mybir.dt.int32
ALU = mybir.AluOpType
ACT = mybir.ActivationFunctionType
AX = mybir.AxisListType

P = 128
D = 1024
SEQ = 1024
KD = D // P
NT = SEQ // P
GROUPS = 4
WINDOWS = (2, 4, 8, 16)
REACH = 16
HALO = (NT - 1) * REACH
EXPERTS = 32
TOPK = 4
SLOTS = 154
TAIL = SLOTS - P
QUARTERS = 4
QW = D // QUARTERS
QP = QUARTERS * TAIL
MORE = -(-SEQ // SLOTS) - 1
OVER = TOPK * SEQ // SLOTS
WIDTHS = (SLOTS, 144, 136, P)
LOOPS = len(WIDTHS)
JOBS = EXPERTS + OVER + LOOPS - 1
LISTS = MORE + LOOPS
CANDIDATES = LISTS * EXPERTS
TABLE = 72
T_ENDS = TABLE - LOOPS
ALPHA = 2.0 ** 0.25
EPS = 1e-5
LIMIT = 7.0
SWIGLU = 1.702
FAR = 4096.0

GU = 8
DN = 4
UNITS = GU + DN
COLS = 256
LOADS = UNITS // 2
RAWS = 3
RING = 4
TILES = 2 * UNITS
HI_AHEAD, LO_AHEAD = 4, 3
POOL_LO = (3, 5)

POOL_STEPS = 11

K_IDENT, K_IOTA, K_TAKE, K_SCALE, K_OWN, K_BOFF = (
    0, P, 2 * P + QP, 2 * P + QP + 2, 2 * P + QP + 4, 2 * P + QP + 6)
K_END = K_BOFF + MORE + 2
C_BAND, C_FIRST, C_TRI = 0, GROUPS * P, 2 * GROUPS * P
C_SEG = C_TRI + P
C_LEVEL = C_SEG + NT * EXPERTS
C_UNDER = C_LEVEL + CANDIDATES
C_ECODE = C_UNDER + CANDIDATES
C_BCODE = C_ECODE + CANDIDATES
C_PIDX = C_BCODE + CANDIDATES
C_TOK = C_PIDX + 1
C_END = C_TOK + 3 * NT


def pool_n(job, n):
    return job * POOL_STEPS + n


def lo_count(pool, job, unit):
    own = [u for u in range(UNITS) if (u in POOL_LO) == pool]
    return job * len(own) + len([u for u in own if u <= unit])


def build_program(nc, x, w_mix, mix_scale, ln1, ln2, router_w, router_b, w_gu, w_dn, biases, keep, consts,
                  halo, out):
    x1_rows = nc.dram_tensor("x1_rows", [SEQ + SLOTS, D], F32).ap()
    sum_rows = nc.dram_tensor("sum_rows", [SEQ + SLOTS, D], F32).ap()

    x1_quarters, sum_quarters = (t.rearrange("r (q n) -> (r q) n", n=QW) for t in (x1_rows, sum_rows))

    ctx = ExitStack()
    with ctx:
        def sb(name, shape, dt=F32):
            return ctx.enter_context(nc.sbuf_tensor(name, shape, dt))

        def sem(name):
            return ctx.enter_context(nc.semaphore(name))

        region = 2 * RING * KD * COLS * 4
        sb("region", [P, region // 4])
        region_at = nc.sbuf_base - region

        raw = sb("raw", [P, RAWS, KD, 2 * COLS])
        x_rows = sb("x_rows", [P, 2, D])
        x_parts = sb("x_parts", [P, KD, 2, SLOTS], F32R)
        act = sb("act", [P, KD, SLOTS])
        act_parts = sb("act_parts", [P, KD, 2, SLOTS], F32R)
        half = sb("half", [P, 2, 2, SLOTS])
        inner = sb("inner", [P, 2, 2, SLOTS])
        sig = sb("sig", [P, 2, SLOTS])
        up_gate = sb("up_gate", [P, 2, SLOTS])
        y_cols = sb("y_cols", [P, 2, 2, P])
        y_tail = sb("y_tail", [P, 2, DN, TAIL])
        y_rows = sb("y_rows", [P, 2, D])
        onehot = sb("onehot", [P, NT, P + QP], BF16)
        slot_src = sb("slot_src", [P, NT, 6], BF16)
        slot_val = sb("slot_val", [P, 2, 6])
        rank_col = sb("rank_col", [P, NT])
        tiny = sb("tiny", [P, 5, 2])
        idx_next = sb("idx_next", [P, 2], I32)
        idx_cur = sb("idx_cur", [P, 2], I32)
        gate_next = sb("gate_next", [P, 2])
        gate_cur = sb("gate_cur", [P, 2])
        bias_next = sb("bias_next", [P, 3 * KD])
        bias_cur = sb("bias_cur", [P, 3 * KD])
        rank = sb("rank", [P, NT, EXPERTS])
        gate3 = sb("gate3", [P, NT, EXPERTS, 3], BF16)
        kc = sb("kc", [P, K_END])
        table = sb("table", [1, 2, TABLE], I32)
        ident = kc[:, K_IDENT:K_IDENT + P]

        cc = sb("cc", [P, C_END])
        x1_t = sb("x1_t", [P, 2, D])
        gb1 = sb("gb1", [P, 2, D])
        rw = sb("rw", [P, KD, EXPERTS])
        rb = sb("rb", [EXPERTS, 1])
        tri = sb("tri", [P, 2, P], BF16)
        halo_x = y_rows[0:HALO, 0]
        halo_band = y_rows[0:HALO, 1, 0:GROUPS * HALO].rearrange("p (g n) -> p g n", n=HALO)
        halo_diff = x_rows[:, 0, 0:KD * HALO].rearrange("p (k n) -> p k n", n=HALO)
        mv = sb("mv", [P, 3, 18])
        sum_t = y_rows

        def place(name, shape, dt, offset):
            size = 4
            for n in shape[1:]:
                size *= n
            assert offset + size <= region
            return nc.alloc_sbuf_tensor_at(name, shape, dt, offset=region_at + offset)

        w_hi = place("w_hi", [P, RING, KD, 2, P], F32R, 0)
        w_lo = place("w_lo", [P, RING, KD, 2, P], F32R, region // 2)
        kb = 1024
        x_t = place("x_t", [P, NT, D], F32, 0)
        wm = place("wm", [P, KD, 2 * P], F32, 32 * kb)
        diffs = [place("diff", [P, KD, P], F32, 40 * kb), act[:, :, 0:P]]
        res = place("res", [P, 2, D], F32, 44 * kb)
        x1_cols = place("x1_cols", [P, KD, P], F32, 52 * kb)
        scale_b = place("scale_b", [P, D], F32, 56 * kb)
        fin = place("fin", [P, NT, D], F32, 0)
        gb2 = gb1

        big, eq, cs, sel, ex = (place(n, [P, NT, EXPERTS], F32, (56 + i) * kb)
                                for i, n in enumerate(("big", "eq", "cs", "sel", "ex")))
        lgt = place("lgt", [EXPERTS, P], F32, 62 * kb)
        top = sb("top", [P, NT, 8])
        per = sb("per", [P, 4, NT])
        in_four = sb("in_four", [P, NT, TOPK])
        mask = sb("mask", [P, NT, EXPERTS], BF16)
        cnt = sb("cnt", [P, EXPERTS])
        is_job, nth, term = (place(n, [P, LISTS, EXPERTS], F32, (48 + 2 * i) * kb)
                             for i, n in enumerate(("is_job", "nth", "term")))
        code = sb("code", [P, 2])
        ends = sb("ends", [P, LOOPS])

        pair = [ctx.enter_context(nc.psum_tensor(f"pair{i}", [P, 2, 512], F32)) for i in range(4)]
        bank = [p[:, i] for p in pair for i in range(2)]
        unit_banks, ub, tb, dispatch_bank, rank_bank = pair[0:2], bank[0:4], bank[4:6], bank[6], bank[7]
        tail_bank = rank_bank

        s_keep = sem("s_keep")
        s_band, s_kc, s_wm, s_gb, s_rw = sem("s_band"), sem("s_kc"), sem("s_wm"), sem("s_gb"), sem("s_rw")
        s_halo_in = sem("s_halo_in")
        s_halo, s_haloc = sem("s_halo"), sem("s_haloc")
        s_x = [sem(f"s_x_tile{i}") for i in range(NT)]
        s_scaled = sem("s_scaled")
        s_diff = sem("s_diff")
        s_diffc = sem("s_diffc")
        s_h = sem("s_h")
        s_res = sem("s_res")
        s_dve = sem("s_dve")
        s_var = sem("s_var")
        s_std = sem("s_std")
        s_nrm = sem("s_nrm")
        s_xn = sem("s_xn")
        s_gx = sem("s_gx")
        s_x1 = sem("s_x1")
        s_ax = sem("s_ax")
        s_st = [sem(f"s_st{i}") for i in range(2)]
        s_tr = sem("s_tr")
        s_trc = [sem("s_trc_act"), sem("s_trc_dve")]
        s_lg = sem("s_lg")
        s_lgc = sem("s_lgc")
        s_back = sem("s_back")
        s_ex = sem("s_ex")
        s_mask = sem("s_mask")
        s_rank = sem("s_rank")
        s_route = sem("s_route")
        s_code = sem("s_code")
        s_row = sem("s_row")
        s_tab = sem("s_tab")
        s_zero = sem("s_zero")
        s_apart = sem("s_apart")
        s_init = sem("s_init")

        s_raw = [sem(f"s_raw{i}") for i in range(RAWS)]
        s_hi = sem("s_hi")
        s_lo = [sem("s_lo_dve"), sem("s_lo_pool")]
        s_tile = sem("s_tile")
        s_half = sem("s_half")
        s_out_of = sem("s_out_of")
        s_in = sem("s_in")
        s_ug = sem("s_ug")
        s_sig = sem("s_sig")
        s_act = sem("s_act")
        s_ahi, s_alo = sem("s_ahi"), sem("s_alo")
        s_ytr = sem("s_ytr")
        s_yrow = sem("s_yrow")
        s_col = sem("s_col")
        s_hot = sem("s_hot")
        s_disp = sem("s_disp")
        s_val = sem("s_val")
        s_pool = sem("s_pool")
        s_gat = [sem("s_gat_main"), sem("s_gat_tail")]
        s_xtr = sem("s_xtr")
        s_xhi, s_xlo = sem("s_xhi"), sem("s_xlo")
        s_bias, s_bcur = sem("s_bias"), sem("s_bcur")
        s_sum = [sem("s_sum_main"), sem("s_sum_tail")]
        s_fin = [sem(f"s_fin{i}") for i in range(NT)]
        s_own = sem("s_own")
        s_gb2, s_out = sem("s_gb2"), sem("s_out")

        block = ctx.enter_context(nc.Block())

        def wait(eng, s, value):
            if not isinstance(value, int) or value > 0:
                eng.wait_ge(s, value)

        def apart(eng):
            eng.sem_inc(s_apart, 1)

        def of(job, unit):
            return (job + 1, unit - UNITS) if unit >= UNITS else (job, unit)

        def tile_n(j, u, t):
            return j * TILES + 2 * u + t + 1

        def out_of(j, u):
            return j * UNITS + 2 + u + 1

        def added(j):
            return j * 16 + 32

        def y_turned(j, i):
            return j * 4 + i + 2

        def rows_out(j):
            return j * 3 + 2

        def x_piece(part, piece):
            if piece == 0:
                return x_parts[:, :, part, P:SLOTS].rearrange("p (q h) s -> p h q s", h=2)
            return x_parts[:, 4 * piece - 4:4 * piece, part, 0:P]

        def turned(piece):
            if piece == 0:
                return tail_bank[:, 0:2 * QP].rearrange("p (h q s) -> p h q s", h=2, q=QUARTERS)
            return tb[piece - 1].rearrange("p (k s) -> p k s", k=4)

        def wait_raw(eng, job, unit):
            load = unit // 2
            eng.wait_ge(s_raw[load % RAWS], (job * (LOADS // RAWS) + load // RAWS + 1) * 16)

        def wait_lo(eng, job, unit):
            pool = unit in POOL_LO
            eng.wait_ge(s_lo[pool], lo_count(pool, job, unit))

        def unit_of_raw(t, unit):
            v = t[:, unit // 2 % RAWS, :, unit % 2 * COLS:(unit % 2 + 1) * COLS]
            if unit < GU:
                return v.rearrange("p k (n t) -> p k t n", t=2)
            return v.rearrange("p k (t n) -> p k t n", t=2)

        def lo_part(eng, job, unit):
            eng.wait_ge(s_hi, job * UNITS + unit + 1)
            r = unit % RING
            eng.tensor_tensor(w_lo[:, r], unit_of_raw(raw, unit), w_hi[:, r].bitcast(F32), ALU.subtract)\
               .then_inc(s_lo[unit in POOL_LO], 1)

        @block.sync
        def _(sp):
            def load_weights(e, load):
                slot = load % RAWS
                if load < GU // 2:
                    src = w_gu[e, :, load * 2 * COLS:(load + 1) * 2 * COLS]
                else:
                    src = w_dn[e, :, (load - GU // 2) * 2 * COLS:(load - GU // 2 + 1) * 2 * COLS]
                sp.dma_start(raw[:, slot], src.rearrange("(k p) n -> p k n", p=P)).then_inc(s_raw[slot], 16)

            sp.dma_start(x_t[:, 0], x[0:P, :]).then_inc(s_x[0], 16)
            sp.dma_start(cc[:, 0:C_TRI], consts[:, 0:C_TRI]).then_inc(s_band, 16)
            sp.dma_start(halo_band, halo.rearrange("p (g n) -> p g n", n=HALO)).then_inc(s_halo_in, 16)
            for i in range(NT - 1):
                sp.dma_start(halo_x[i * REACH:(i + 1) * REACH, :], x[(i + 1) * P - REACH:(i + 1) * P, :])\
                  .then_inc(s_halo_in, 16)
            sp.dma_start(kc[:, :], keep).then_inc(s_keep, 16)
            sp.dma_start(x_t[:, 1], x[P:2 * P, :]).then_inc(s_x[1], 16)
            sp.dma_start(wm[:, :, :], w_mix.rearrange("(k p) n -> p k n", p=P)).then_inc(s_wm, 16)
            sp.dma_start(scale_b[:, :], mix_scale.to_broadcast((P, D))).then_inc(s_wm, 16)
            sp.dma_start(x_t[:, 2], x[2 * P:3 * P, :]).then_inc(s_x[2], 16)
            sp.dma_start(cc[:, C_TRI:C_END], consts[:, C_TRI:C_END]).then_inc(s_kc, 16)
            for i in range(2):
                sp.dma_start(gb1[:, i], ln1[i:i + 1, :].to_broadcast((P, D))).then_inc(s_gb, 16)
            sp.dma_start(rw[:, :, :], router_w.rearrange("(k p) n -> p k n", p=P)).then_inc(s_rw, 16)
            sp.dma_start(rb[:, :], router_b.rearrange("o e -> e o")).then_inc(s_rw, 16)
            for i in range(3, NT):
                sp.dma_start(x_t[:, i], x[i * P:(i + 1) * P, :]).then_inc(s_x[i], 16)
            sp.wait_ge(s_zero, 1)
            zeros = x_rows[:, 1]
            sp.dma_start(x1_rows[SEQ:SEQ + P, :], zeros).then_inc(s_own, 16)
            sp.dma_start(x1_rows[SEQ + P:SEQ + SLOTS, :], zeros[0:TAIL]).then_inc(s_own, 16)
            load_weights(0, 0)
            sp.dma_start(bias_next[:, :], biases[0]).then_inc(s_bias, 16)
            for i in range(NT):
                sp.wait_ge(s_x1, i + 1)
                sp.dma_start(x1_rows[i * P:(i + 1) * P, :], x1_t[:, i % 2]).then_inc(s_st[i % 2], 16)
                sp.wait_ge(s_ax, i + 1)
                sp.dma_start(sum_rows[i * P:(i + 1) * P, :], sum_t[:, i % 2]).then_inc(s_st[i % 2], 16)
                if i in (1, 3):
                    load_weights(0, i // 2 + 1)
            for i in range(2):
                sp.dma_start(gb2[:, i], ln2[i:i + 1, :].to_broadcast((P, D))).then_inc(s_gb2, 16)
            sp.wait_ge(s_tab, 2)
            jobs = sp.value_load(table[0:1, 0, TABLE - 1:TABLE], min_val=EXPERTS, max_val=JOBS)
            with sp.Fori(0, jobs) as j:
                for q in range(LOADS):
                    if q % RAWS == 0:
                        nxt = q // RAWS
                        e = sp.value_load(table[0:1, 0, bass.ds(j + nxt, 1)], min_val=0, max_val=EXPERTS - 1)
                    for unit in (2 * q, 2 * q + 1):
                        wait_lo(sp, j, unit)
                        apart(sp)
                    load_weights(e, (q + RAWS) % LOADS)
                    if q == RAWS:
                        sp.wait_ge(s_bcur, j * 3 + 3)
                        apart(sp)
                        sp.dma_start(bias_next[:, :], biases[e]).then_inc(s_bias, 16)
            for s in s_sum:
                sp.wait_ge(s, added(jobs))
                apart(sp)
            sp.wait_ge(s_hi, jobs * UNITS + HI_AHEAD)
            apart(sp)
            sp.wait_ge(s_lo[0], lo_count(False, jobs, LO_AHEAD - 1))
            apart(sp)
            sp.wait_ge(s_tile, jobs * TILES)
            apart(sp)
            for i in range(NT):
                sp.dma_start(fin[:, i], sum_rows[i * P:(i + 1) * P, :]).then_inc(s_fin[i], 16)
            for i in range(NT):
                sp.wait_ge(s_x1, NT + i + 1)
                sp.dma_start(out[i * P:(i + 1) * P, :], fin[:, i]).then_inc(s_out, 16)
            sp.wait_ge(s_out, 16 * NT)
            for i in range(RAWS):
                sp.wait_ge(s_raw[i], jobs * (LOADS // RAWS) * 16 + 16)
            apart(sp)
            sp.wait_ge(s_bias, jobs * 16 + 16)
            apart(sp)

        @block.tensor
        def _(pe):
            def windows(i):
                pe.wait_ge(s_x[i], 16)
                for half in range(2):
                    if i > 0:
                        pe.wait_ge(s_diffc, 2 * i - 1 + half)
                    for c in range(4 * half, 4 * half + 4):
                        b = (C_FIRST if i == 0 else C_BAND) + c // 2 * P
                        last = pe.matmul(ub[half][:, c % 4 * P:(c % 4 + 1) * P], x_t[:, i, c * P:(c + 1) * P],
                                         cc[:, b:b + P], start=c % 4 == 0, stop=i == 0 and c % 4 == 3,
                                         skip_group_check=True)
                    if i > 0:
                        last = pe.matmul(ub[half].rearrange("p (c n) -> p c n", n=P)[:, :, 0:REACH], ident,
                                         halo_diff[:, 4 * half:4 * half + 4, (i - 1) * REACH:i * REACH],
                                         start=False, stop=True, skip_group_check=True)
                    last.then_inc(s_diff, 1)

            def halo_windows():
                pe.wait_ge(s_halo_in, NT * 16)
                for c in range(KD):
                    last = pe.matmul(tb[c // 4][:, c % 4 * HALO:(c % 4 + 1) * HALO], halo_x[:, c * P:(c + 1) * P],
                                     halo_band[:, c // 2], start=True, stop=True)
                last.then_inc(s_halo, 1)

            def mix(i):
                for half in range(2):
                    pe.wait_ge(s_diffc, 2 * i + half + 1)
                    if i > 0:
                        pe.wait_ge(s_res, 2 * i - 1 + half)
                    for g in (2 * half, 2 * half + 1):
                        for k in range(2):
                            last = pe.matmul(ub[2 + half][:, g % 2 * 256:(g % 2 + 1) * 256],
                                             diffs[i % 2][:, 2 * g + k], wm[:, 2 * g + k], start=k == 0, stop=k == 1)
                    last.then_inc(s_h, 1)

            def turn_x1(i):
                pe.wait_ge(s_x1, i + 1)
                for half in range(2):
                    if i > 0:
                        pe.wait_ge(s_trc[half], i)
                    for c in range(4):
                        k = 4 * half + c
                        last = pe.transpose(tb[half][:, c * P:(c + 1) * P], x1_t[:, i % 2, k * P:(k + 1) * P], ident)
                    last.then_inc(s_tr, 1)

            def logits(i):
                if i > 0:
                    pe.wait_ge(s_lgc, i)
                for k in range(KD):
                    if k % 4 == 0:
                        pe.wait_ge(s_trc[k // 4], i + 1)
                    last = pe.matmul(rank_bank[0:EXPERTS, 0:P], rw[:, k], x1_cols[:, k],
                                     start=k == 0, stop=k == KD - 1)
                last.then_inc(s_lg, 1)

            def turn_logits(i):
                pe.wait_ge(s_lgc, i + 1)
                pe.transpose(dispatch_bank[:, i * EXPERTS:(i + 1) * EXPERTS], lgt[:, :], ident[0:EXPERTS, 0:EXPERTS])\
                  .then_inc(s_back, 1)

            pe.wait_ge(s_band, 16)
            windows(0)
            halo_windows()
            pe.wait_ge(s_keep, 16)
            pe.wait_ge(s_haloc, 1)
            windows(1)
            pe.wait_ge(s_scaled, 1)
            mix(0)
            for i in range(1, NT + 3):
                if i + 1 < NT:
                    windows(i + 1)
                if 2 <= i < NT + 2:
                    turn_x1(i - 2)
                if i < NT:
                    mix(i)
                if i >= 3:
                    turn_logits(i - 3)
                if i == 2:
                    pe.wait_ge(s_rw, 32)
                if 2 <= i < NT + 2:
                    logits(i - 2)
            pe.wait_ge(s_zero, 6)
            pe.wait_ge(s_mask, 1)
            r = rank_bank[:, 0:NT * EXPERTS]
            pe.matmul(r, tri[:, 0], mask[:, :, :].rearrange("p a b -> p (a b)"), start=True, stop=False)
            for i in range(NT - 1):
                o = rank_bank[:, (i + 1) * EXPERTS:NT * EXPERTS]
                pe.matmul(o, tri[:, 1], mask[:, i:i + 1].to_broadcast((P, NT - 1 - i, EXPERTS)),
                          start=False, stop=i == NT - 2)
            for i in range(NT):
                last = pe.matmul(rank_bank[:, 256:256 + EXPERTS], tri[:, 1], mask[:, i], start=i == 0, stop=i == NT - 1,
                                 skip_group_check=True)
            last.then_inc(s_rank, 1)

            def dispatch(job):
                pe.wait_ge(s_hot, job + 1)
                wait(pe, s_val, job)
                for part, m in ((0, P), (1, QP)):
                    for i in range(NT):
                        last = pe.matmul(dispatch_bank[0:m, 8 * part:8 * part + 6], onehot[:, i, part * P:part * P + m],
                                         slot_src[:, i], start=i == 0, stop=i == NT - 1)
                last.then_inc(s_disp, 1)

            def turn_x(job):
                for s in s_gat:
                    pe.wait_ge(s, job * 16 + 16)
                if not isinstance(job, int):
                    pe.wait_ge(s_yrow, rows_out(job - 1))
                for h in range(2):
                    last = pe.transpose(tail_bank[:, h * QP:(h + 1) * QP], x_rows[0:QP, 1, h * P:(h + 1) * P],
                                        ident[0:QP, 0:QP])
                last.then_inc(s_xtr, 1)
                for piece in range(2):
                    for c in range(4):
                        k = 4 * piece + c
                        last = pe.transpose(tb[piece][:, c * P:(c + 1) * P], x_rows[:, 0, k * P:(k + 1) * P], ident)
                    last.then_inc(s_xtr, 1)

            def turn_y(j, i):
                pe.wait_ge(s_out_of, out_of(j, GU + i))
                if i == 0:
                    pe.wait_ge(s_xlo, j * 3 + 6)
                for t in range(2):
                    c = (2 * i + t) % 4 * P
                    last = pe.transpose(tb[i // 2][:, c:c + P], y_cols[:, i % 2, t], ident)
                if i == DN - 1:
                    for h in range(2):
                        last = pe.transpose(tail_bank[0:QP, h * P:(h + 1) * P],
                                            y_tail[:, h].rearrange("p q s -> p (q s)"), ident)
                last.then_inc(s_ytr, 1)

            def products(j, u, width):
                pe.wait_ge(s_hi, j * UNITS + u + 1)
                wait_lo(pe, j, u)
                parts = x_parts if u < GU else act_parts
                r = u % RING
                pe.wait_ge(s_out_of, out_of(j, u - 2))
                order = [(t, k) for t in range(2) for k in range(KD)]
                if u == GU:
                    order.sort(key=lambda tk: max(tk[1], KD - 3))
                for n, (t, k) in enumerate(order):
                    o = ub[u % 2 * 2 + t]
                    if u == GU and t == 0 and k in (0, KD - 2, KD - 1):
                        chunks = j * GU + max(k + 1, KD - 2)
                        pe.wait_ge(s_ahi, chunks)
                        pe.wait_ge(s_alo, chunks)
                    if u == 0 and t == 0 and k % 4 == 0:
                        pe.wait_ge(s_xlo, j * 3 + k // 4 + 2)
                    for lo in ((0, 1) if k == 0 else (1, 0)):
                        if lo:
                            pe.matmul(o[:, SLOTS:SLOTS + width], w_lo[:, r, k, t], parts[:, k, 0, 0:width],
                                      start=False, stop=False)
                        else:
                            last = pe.matmul(o[:, 0:2 * SLOTS].rearrange("p (a s) -> p a s", a=2)[:, :, 0:width],
                                             w_hi[:, r, k, t], parts[:, k, :, 0:width],
                                             start=k == 0, stop=k == KD - 1)
                    if k == KD - 1:
                        last.then_inc(s_tile, 1)

            pe.wait_ge(s_route, 1)
            pe.wait_ge(s_res, 2 * NT)
            pe.wait_ge(s_diffc, 2 * NT)
            dispatch(0)
            pe.wait_ge(s_code, 1)
            for n in range(2):
                last = pe.matmul(rank_bank[0:1, n * P:(n + 1) * P], code[:, n:n + 1], ident, start=True, stop=True)
            last.then_inc(s_row, 1)
            pe.wait_ge(s_tab, 2)
            turn_x(0)
            jobs = pe.value_load(table[0:1, 0, TABLE - 1:TABLE], min_val=EXPERTS, max_val=JOBS)
            starts = [0] + [pe.value_load(table[0:1, 0, T_ENDS + n:T_ENDS + n + 1], min_val=n + 1, max_val=JOBS)
                            for n in range(LOOPS - 1)]

            def run_job(j, width):
                for u in range(UNITS):
                    products(j, u, width)
                    if u == 0:
                        turn_y(j - 1, DN - 1)
                    if u == 2:
                        dispatch(j + 1)
                    if u == GU - 1:
                        turn_x(j + 1)
                    if u > GU:
                        turn_y(j, u - GU - 1)

            for width, start, end in zip(WIDTHS, starts, starts[1:] + [jobs]):
                with pe.Fori(start, end) as j:
                    run_job(j, width)
            turn_y(jobs - 1, DN - 1)

        @block.scalar
        def _(ac):
            def hi_part(job, unit):
                wait_raw(ac, job, unit)
                ac.activation(w_hi[:, unit % RING], unit_of_raw(raw, unit), ACT.Copy).then_inc(s_hi, 1)

            def copy_diff(i):
                for half in range(2):
                    ac.wait_ge(s_diff, 2 * i + half + 1)
                    if i > 1:
                        ac.wait_ge(s_h, 2 * i - 3 + half)
                    ac.activation(diffs[i % 2][:, 4 * half:4 * half + 4], ub[half].rearrange("p (a b) -> p a b", b=P),
                                  ACT.Copy).then_inc(s_diffc, 1)

            def normalise(n, src):
                ac.wait_ge(s_var, n + 1)
                m = mv[:, n % 3]
                ac.activation(m[:, 15:16], m[:, 14:15], ACT.Sqrt).then_inc(s_std, 1)
                ac.wait_ge(s_nrm, n + 1)
                ac.activation(src, src, ACT.Identity, scale=m[:, 16:17], bias=m[:, 17:18]).then_inc(s_xn, 1)

            def store_sum(i):
                ac.wait_ge(s_x1, i + 1)
                if i >= 2:
                    ac.wait_ge(s_st[i % 2], i // 2 * 32)
                ac.activation(sum_t[:, i % 2], x1_t[:, i % 2], ACT.Copy, scale=ALPHA).then_inc(s_ax, 1)

            def copy_x1(i):
                ac.wait_ge(s_tr, 2 * i + 1)
                if i > 0:
                    ac.wait_ge(s_lg, i)
                ac.activation(x1_cols[:, 0:4].rearrange("p a b -> p (a b)"), tb[0], ACT.Copy)\
                  .then_inc(s_trc[0], 1)

            def copy_logits(i):
                ac.wait_ge(s_lg, i + 1)
                if i > 0:
                    ac.wait_ge(s_back, i)
                else:
                    ac.wait_ge(s_rw, 32)
                ac.activation(lgt[:, :], rank_bank[0:EXPERTS, 0:P], ACT.Identity, bias=rb[:, :]).then_inc(s_lgc, 1)

            copy_diff(0)
            copy_diff(1)
            for i in range(1, NT + 3):
                if i >= 3:
                    copy_logits(i - 3)
                if i + 1 < NT:
                    copy_diff(i + 1)
                if i <= NT:
                    normalise(i - 1, res[:, (i - 1) % 2])
                if 2 <= i < NT + 2:
                    copy_x1(i - 2)
                    store_sum(i - 2)
                unit = i // 2 - 1
                if i % 2 == 0 and unit < HI_AHEAD:
                    ac.wait_ge(s_res, 2 * (2 * unit + 2))
                    hi_part(0, unit)
            ac.wait_ge(s_ex, 1)
            ac.activation(ex[:, :, :], ex[:, :, :], ACT.Exp).then_inc(s_ex, 1)

            def copy_x(job):
                for piece in range(3):
                    ac.wait_ge(s_xtr, job * 3 + piece + 1)
                    ac.activation(x_piece(0, piece), turned(piece), ACT.Copy).then_inc(s_xhi, 1)

            def y_out(j, half):
                ac.wait_ge(s_ytr, y_turned(j, 2 * half + 1))
                if half == 0:
                    ac.wait_ge(s_pool, pool_n(j + 1, 3))
                    for s in s_sum:
                        ac.wait_ge(s, added(j))
                ac.activation(y_rows[:, 0, half * 512:half * 512 + 512], tb[half], ACT.Copy,
                              scale=gate_cur[:, 0:1]).then_inc(s_yrow, 1)
                if half == 1:
                    ac.activation(y_rows[0:QP, 1, 0:QW], tail_bank[0:QP, 0:QW], ACT.Copy,
                                  scale=gate_cur[0:QP, 1:2]).then_inc(s_yrow, 1)

            copy_x(0)
            for s in s_st:
                ac.wait_ge(s, NT // 2 * 32)
            ac.wait_ge(s_pool, 3)
            ac.wait_ge(s_tab, 2)
            jobs = ac.value_load(table[0:1, 0, TABLE - 1:TABLE], min_val=EXPERTS, max_val=JOBS)
            with ac.Fori(0, jobs) as j:
                def split_act(u):
                    ac.wait_ge(s_act, j * GU + u + 1)
                    ac.activation(act_parts[:, u, 0], act[:, u], ACT.Copy).then_inc(s_ahi, 1)

                def second_half(u, t):
                    ac.wait_ge(s_tile, tile_n(j, u, t))
                    b = t * KD + u if u < GU else 2 * KD + 2 * (u - GU) + t
                    ac.activation(half[:, u % 2, t], ub[u % 2 * 2 + t][:, SLOTS:2 * SLOTS],
                                  ACT.Identity, bias=bias_cur[:, b:b + 1]).then_inc(s_half, 1)

                def gate_sigmoid(u):
                    ac.wait_ge(s_in, j * 2 * GU + 2 * u + 1)
                    ac.activation(sig[:, u % 2], inner[:, u % 2, 0], ACT.Sigmoid, scale=SWIGLU).then_inc(s_sig, 1)

                ac.activation(tiny[:, 3, 1:2], kc[:, 0:1], ACT.Sigmoid)
                ac.wait_ge(s_bcur, j * 3 + 3)
                for u in range(UNITS):
                    if u == GU:
                        copy_x(j + 1)
                    if u == UNITS - 1:
                        y_out(j, 0)
                    second_half(u, 0)
                    second_half(u, 1)
                    if 0 < u < GU:
                        split_act(u - 1)
                    if u == GU - 1:
                        gate_sigmoid(u)
                        split_act(u)
                    hi_part(*of(j, u + HI_AHEAD))
                    if u < GU - 1:
                        gate_sigmoid(u)
                    if u == 0:
                        y_out(j - 1, 1)
            y_out(jobs - 1, 1)
            for i in range(NT):
                normalise(NT + i, fin[:, i])

        @block.vector
        def _(ve):
            done = [0]

            def then_wait(ins):
                done[0] += 1
                ins.then_inc(s_dve, 1)
                ve.wait_ge(s_dve, done[0])

            def norm_stats(n, halves):
                m = mv[:, n % 3]
                for half in range(2):
                    last = ve.bn_stats(m[:, 6 * half:6 * half + 6], halves[half])
                then_wait(last)
                then_wait(ve.bn_aggr(m[:, 12:14], m[:, 0:12]))
                ve.tensor_scalar(m[:, 14:15], m[:, 13:14], EPS, None, ALU.add).then_inc(s_var, 1)

            def norm_scale(n):
                m = mv[:, n % 3]
                ve.wait_ge(s_std, n + 1)
                then_wait(ve.reciprocal(m[:, 16:17], m[:, 15:16]))
                ve.tensor_scalar(m[:, 17:18], m[:, 12:13], m[:, 16:17], -1.0, ALU.mult, ALU.mult).then_inc(s_nrm, 1)

            ve.memset(x_rows[:, 1], 0.0).then_inc(s_zero, 1)
            ve.memset(y_cols[:, 1], 0.0).then_inc(s_zero, 1)
            ve.memset(y_tail[:, :, :, :], 0.0).then_inc(s_zero, 1)
            ve.wait_ge(s_halo, 1)
            for h in range(2):
                last = ve.tensor_copy(halo_diff[:, 4 * h:4 * h + 4],
                                      tb[h][:, 0:4 * HALO].rearrange("p (k n) -> p k n", n=HALO))
            last.then_inc(s_haloc, 1)
            ve.wait_ge(s_wm, 32)
            ve.tensor_tensor(wm[:, :, :].rearrange("p (g k) n -> p g k n", k=2),
                             wm[:, :, :].rearrange("p (g k) n -> p g k n", k=2),
                             scale_b[:, :].rearrange("p (g o n) -> p g o n", g=GROUPS, o=1)
                             .to_broadcast((P, GROUPS, 2, 256)), ALU.mult).then_inc(s_scaled, 1)

            def fixed_parts():
                ve.wait_ge(s_kc, 16)
                ve.wait_ge(s_keep, 16)
                ve.tensor_copy(tri[:, 0], cc[:, C_TRI:C_TRI + P]).then_inc(s_zero, 1)
                ve.memset(tri[:, 1], 1.0).then_inc(s_zero, 1)
                ve.tensor_copy(slot_src[:, :, 0:3],
                               cc[:, C_TOK:C_TOK + 3 * NT].rearrange("p (i c) -> p i c", c=3)).then_inc(s_zero, 1)

            def residual(i):
                ve.wait_ge(s_x[i], 16)
                if i >= 2:
                    ve.wait_ge(s_gx, i - 1)
                for half in range(2):
                    ve.wait_ge(s_h, 2 * i + half + 1)
                    cols = slice(half * 512, half * 512 + 512)
                    ve.scalar_tensor_tensor(res[:, i % 2, cols], x_t[:, i, cols], ALPHA, ub[2 + half],
                                            ALU.mult, ALU.add).then_inc(s_res, 1)
                ve.wait_ge(s_res, 2 * i + 2)
                norm_stats(i, [res[:, i % 2, 0:512], res[:, i % 2, 512:1024]])

            def times_g(i):
                ve.wait_ge(s_xn, i + 1)
                if i >= 2:
                    ve.wait_ge(s_st[i % 2], i // 2 * 32)
                    ve.wait_ge(s_tr, 2 * i - 2)
                    ve.wait_ge(s_ax, i - 1)
                ve.tensor_tensor(x1_t[:, i % 2], res[:, i % 2], gb1[:, 0], ALU.mult).then_inc(s_gx, 1)

            def copy_x1(i):
                ve.wait_ge(s_tr, 2 * i + 2)
                if i > 0:
                    ve.wait_ge(s_lg, i)
                ve.tensor_copy(x1_cols[:, 4:8].rearrange("p a b -> p (a b)"), tb[1]).then_inc(s_trc[1], 1)

            residual(0)
            fixed_parts()
            ve.wait_ge(s_gb, 32)
            for i in range(1, NT + 2):
                if i <= NT:
                    norm_scale(i - 1)
                if i >= 2:
                    copy_x1(i - 2)
                if i <= NT:
                    times_g(i - 1)
                if i < NT:
                    residual(i)
                if i == NT:
                    lo_part(ve, 0, 0)
            lo_part(ve, 0, 1)

            ve.wait_ge(s_back, NT)
            logits = dispatch_bank[:, 0:NT * EXPERTS].rearrange("p (i e) -> p i e", e=EXPERTS)
            whole = (P, NT, EXPERTS)
            for i in range(NT):
                last = ve.max(top[:, i], logits[:, i])
            then_wait(last)
            fourth = top[:, :, TOPK - 1:TOPK]
            ve.tensor_tensor(eq[:, :, :], logits, fourth.to_broadcast(whole), ALU.is_equal)
            then_wait(ve.tensor_tensor(in_four[:, :, :], top[:, :, 0:TOPK], fourth.to_broadcast((P, NT, TOPK)),
                                       ALU.is_equal))
            ve.tensor_tensor(ex[:, :, :], logits, top[:, :, 0:1].to_broadcast(whole), ALU.subtract).then_inc(s_ex, 1)
            line = lambda t: t[:, :, :].rearrange("p i e -> p (i e)")
            ve.tensor_reduce(per[:, 1], in_four[:, :, :], AX.X, ALU.add)
            then_wait(ve.tensor_tensor_scan(line(cs), cc[:, C_SEG:C_SEG + NT * EXPERTS], line(eq), 0.0, ALU.mult, ALU.add))
            ve.tensor_tensor(big[:, :, :], logits, fourth.to_broadcast(whole), ALU.is_gt)
            then_wait(ve.tensor_tensor(cs[:, :, :], cs[:, :, :],
                                       per[:, 1].rearrange("p (i o) -> p i o", o=1).to_broadcast(whole), ALU.is_le))
            then_wait(ve.tensor_tensor(cs[:, :, :], cs[:, :, :], eq[:, :, :], ALU.mult))
            ve.tensor_tensor(mask[:, :, :], cs[:, :, :], big[:, :, :], ALU.add).then_inc(s_mask, 1)
            ve.wait_ge(s_mask, 1)
            ve.wait_ge(s_ex, 2)
            ve.tensor_tensor(ex[:, :, :], ex[:, :, :], mask[:, :, :], ALU.mult)
            then_wait(ve.tensor_scalar(sel[:, :, :], mask[:, :, :], -FAR, FAR, ALU.mult, ALU.add))
            then_wait(ve.tensor_reduce(per[:, 2], ex[:, :, :], AX.X, ALU.add))
            then_wait(ve.reciprocal(per[:, 3], per[:, 2]))
            then_wait(ve.tensor_tensor(ex[:, :, :], ex[:, :, :],
                                       per[:, 3].rearrange("p (i o) -> p i o", o=1).to_broadcast(whole), ALU.mult))
            part = lambda n: gate3[:, :, :, n:n + 1].rearrange("p i e o -> p i (e o)")
            for n in range(2):
                then_wait(ve.tensor_copy(part(n), ex[:, :, :]))
                then_wait(ve.tensor_tensor(ex[:, :, :], ex[:, :, :], part(n), ALU.subtract))
            then_wait(ve.tensor_copy(part(2), ex[:, :, :]))
            ve.wait_ge(s_rank, 1)
            then_wait(ve.tensor_tensor(rank[:, :, :], sel[:, :, :],
                                       rank_bank[:, 0:NT * EXPERTS].rearrange("p (i e) -> p i e", e=EXPERTS), ALU.add))
            then_wait(ve.tensor_copy(cnt[:, :], rank_bank[:, 256:256 + EXPERTS]))
            ve.tensor_copy(per[:, 0, 0:1], rank[:, 0, 0:1]).then_inc(s_route, 1)

            def hot(job):
                ve.wait_ge(s_col, job + 1)
                if not (isinstance(job, int) and job == 0):
                    ve.wait_ge(s_disp, job)
                shape = (P, NT, P + QP)
                ve.tensor_tensor(onehot[:, :, :],
                                 rank_col[:, :].rearrange("p (i o) -> p i o", o=1).to_broadcast(shape),
                                 kc[:, K_IOTA:K_IOTA + P + QP].rearrange("p (o s) -> p o s", o=1).to_broadcast(shape),
                                 ALU.is_equal).then_inc(s_hot, 1)

            def slot_values(job):
                ve.wait_ge(s_disp, job + 1)
                if not (isinstance(job, int) and job == 0):
                    ve.wait_ge(s_pool, pool_n(job - 1, 9))
                ve.tensor_copy(slot_val[:, :, :],
                               dispatch_bank[:, 0:16].rearrange("p (c n) -> p c n", n=8)[:, :, 0:6]).then_inc(s_val, 1)

            def x_lo_part(job):
                for piece in range(3):
                    ve.wait_ge(s_xhi, job * 3 + piece + 1)
                    ve.tensor_tensor(x_piece(1, piece), turned(piece), x_piece(0, piece).bitcast(F32), ALU.subtract)\
                      .then_inc(s_xlo, 1)

            ve.tensor_copy(tiny[:, 4, 0:1], kc[:, 0:1]).then_inc(s_out_of, 2)
            hot(0)
            lists = (P, LISTS, EXPERTS)
            flat = lambda t: t[:, :, :].rearrange("p l e -> p (l e)")
            of_consts = lambda c: cc[:, c:c + CANDIDATES].rearrange("p (l e) -> p l e", e=EXPERTS)
            tokens = cnt[:, :].rearrange("p (o e) -> p o e", o=1).to_broadcast(lists)
            ve.tensor_tensor(is_job[:, :, :], tokens, of_consts(C_LEVEL), ALU.is_gt)
            then_wait(ve.tensor_tensor(term[:, :, :], tokens, of_consts(C_UNDER), ALU.is_gt))
            then_wait(ve.tensor_tensor(is_job[:, :, :], is_job[:, :, :], term[:, :, :], ALU.subtract))
            slot_values(0)
            then_wait(ve.memset(flat(term), 1.0))
            then_wait(ve.tensor_tensor_scan(flat(nth), flat(term), flat(is_job), 0.0, ALU.mult, ALU.add))
            for n in range(LOOPS):
                at = (MORE + n + 1) * EXPERTS
                last = ve.tensor_copy(ends[:, n:n + 1], flat(nth)[:, at - 1:at])
            then_wait(last)
            then_wait(ve.tensor_scalar(flat(nth), flat(nth), cc[:, C_PIDX:C_PIDX + 1], None, ALU.is_equal))
            then_wait(ve.tensor_tensor(flat(is_job), flat(is_job), flat(nth), ALU.mult))
            for n, c in ((0, C_ECODE), (1, C_BCODE)):
                then_wait(ve.tensor_tensor(flat(term), flat(is_job), cc[:, c:c + CANDIDATES], ALU.mult))
                then_wait(ve.tensor_reduce(code[:, n:n + 1], flat(term), AX.X, ALU.add))
            ve.tensor_scalar(code[:, 1:2], code[:, 1:2], float(MORE + 1), None, ALU.add).then_inc(s_code, 1)
            for n in range(1, LOOPS):
                then_wait(ve.tensor_scalar(per[:, 0, 0:1], ends[:, n - 1:n], 1.0, None, ALU.add))
                then_wait(ve.tensor_tensor(ends[:, n:n + 1], ends[:, n:n + 1], per[:, 0, 0:1], ALU.max))
            ve.wait_ge(s_row, 1)
            ve.tensor_copy(table[0:1, :, 0:T_ENDS],
                           rank_bank[0:1, 0:2 * P].rearrange("p (n o) -> p n o", n=2)[:, :, 0:T_ENDS]).then_inc(s_tab, 1)
            ve.tensor_copy(table[0:1, 0, T_ENDS:TABLE], ends[0:1, :]).then_inc(s_tab, 1)
            x_lo_part(0)
            lo_part(ve, 0, LO_AHEAD - 1)
            ve.wait_ge(s_tab, 2)
            jobs = ve.value_load(table[0:1, 0, TABLE - 1:TABLE], min_val=EXPERTS, max_val=JOBS)
            with ve.Fori(0, jobs) as j:
                def lo_next(u):
                    job, unit = of(j, u + LO_AHEAD)
                    if unit not in POOL_LO:
                        lo_part(ve, job, unit)

                def whole(u, *to):
                    ve.wait_ge(s_half, tile_n(j, u, 1))
                    at = 0
                    for t in to:
                        cols = slice(at, at + t.shape[-1])
                        last = ve.tensor_tensor(t, unit_banks[u % 2][:, :, cols], half[:, u % 2, :, cols], ALU.add)
                        at += t.shape[-1]
                    last.then_inc(s_out_of, 1)

                ve.wait_ge(s_bias, j * 16 + 16)
                ve.tensor_copy(bias_cur[:, 0:KD], bias_next[:, 0:KD]).then_inc(s_bcur, 1)
                ve.tensor_copy(bias_cur[:, 2 * KD:3 * KD], bias_next[:, 2 * KD:3 * KD]).then_inc(s_bcur, 1)
                ve.tensor_scalar(bias_cur[:, KD:2 * KD], bias_next[:, KD:2 * KD], 1.0, None, ALU.add).then_inc(s_bcur, 1)
                for u in range(UNITS):
                    if u == 3:
                        slot_values(j + 1)
                    if u == GU:
                        x_lo_part(j + 1)
                    if u < GU:
                        g, v = inner[:, u % 2, 0], inner[:, u % 2, 1]
                        whole(u, inner[:, u % 2])
                        ve.wait_ge(s_out_of, out_of(j, u))
                        ve.tensor_scalar(g, g, LIMIT, None, ALU.min).then_inc(s_in, 1)
                        ve.tensor_scalar(v, v, 1.0 + LIMIT, 1.0 - LIMIT, ALU.min, ALU.max).then_inc(s_in, 1)
                        ve.wait_ge(s_in, j * 2 * GU + 2 * u + 2)
                        ve.tensor_tensor(up_gate[:, u % 2], v, g, ALU.mult).then_inc(s_ug, 1)
                        if u < GU - 1:
                            lo_next(u)
                        if u == 0:
                            hot(j + 1)
                        ve.wait_ge(s_sig, j * GU + u + 1)
                        ve.wait_ge(s_ug, j * GU + u + 1)
                        ve.tensor_tensor(act[:, u], up_gate[:, u % 2], sig[:, u % 2], ALU.mult).then_inc(s_act, 1)
                    else:
                        i = u - GU
                        ve.wait_ge(s_ytr, y_turned(j, i - 2) if i >= 2 else y_turned(j - 1, DN - 1))
                        whole(u, y_cols[:, i % 2], y_tail[:, :, i])
                    if u >= GU - 1:
                        lo_next(u)
            ve.wait_ge(s_gb2, 32)
            def mark(ins):
                done[0] += 1
                ins.then_inc(s_dve, 1)
                return done[0]

            for i in range(NT + 2):
                m, before = mv[:, (NT + i) % 3], mv[:, (NT + i - 1) % 3]
                if i < NT:
                    ve.wait_ge(s_fin[i], 16)
                    ve.bn_stats(m[:, 0:6], fin[:, i, 0:512])
                    stats = mark(ve.bn_stats(m[:, 6:12], fin[:, i, 512:1024]))
                if i > 1:
                    ve.wait_ge(s_xn, NT + i - 1)
                    ve.tensor_tensor(fin[:, i - 2], fin[:, i - 2], gb2[:, 0], ALU.mult).then_inc(s_gx, 1)
                if i < NT:
                    ve.wait_ge(s_dve, stats)
                    variance = mark(ve.bn_aggr(m[:, 12:14], m[:, 0:12]))
                if 0 < i <= NT:
                    ve.wait_ge(s_std, NT + i)
                    inverse = mark(ve.reciprocal(before[:, 16:17], before[:, 15:16]))
                if i < NT:
                    ve.wait_ge(s_dve, variance)
                    ve.tensor_scalar(m[:, 14:15], m[:, 13:14], EPS, None, ALU.add).then_inc(s_var, 1)
                if 0 < i <= NT:
                    ve.wait_ge(s_dve, inverse)
                    ve.tensor_scalar(before[:, 17:18], before[:, 12:13], before[:, 16:17], -1.0, ALU.mult, ALU.mult)\
                      .then_inc(s_nrm, 1)

        @block.gpsimd
        def _(po):
            po.wait_ge(s_zero, 1)
            for part, m in ((0, P), (1, TAIL)):
                po.dma_start(sum_rows[SEQ + part * P:SEQ + part * P + m, :], x_rows[0:m, 1]).then_inc(s_sum[part], 16)
            po.wait_ge(s_gb, 32)
            for i in range(NT):
                po.wait_ge(s_gx, i + 1)
                po.tensor_tensor(x1_t[:, i % 2], x1_t[:, i % 2], gb1[:, 1], ALU.add).then_inc(s_x1, 1)
            po.wait_ge(s_kc, 16)
            po.wait_ge(s_keep, 16)
            po.wait_ge(s_zero, 6)

            def columns(job, e, b):
                if not (isinstance(job, int) and job == 0):
                    po.wait_ge(s_disp, job)
                    apart(po)
                po.tensor_copy(slot_src[:, :, 3:6], gate3[:, :, bass.ds(e, 1), :].rearrange("p i o n -> p i (o n)"))\
                  .then_inc(s_pool, 1)
                po.wait_ge(s_pool, pool_n(job, 1))
                po.tensor_tensor(rank_col[:, :].rearrange("p (i o) -> p i o", o=1), rank[:, :, bass.ds(e, 1)],
                                 kc[:, bass.ds(K_BOFF + b, 1)].rearrange("p (a o) -> p a o", o=1).to_broadcast((P, NT, 1)),
                                 ALU.subtract).then_inc(s_col, 1)

            def rows(job):
                n = [1]

                def count(*instructions):
                    for ins in instructions:
                        n[0] += 1
                        ins.then_inc(s_pool, 1)
                    po.wait_ge(s_pool, pool_n(job, n[0]))
                    apart(po)

                if not isinstance(job, int):
                    for s in s_sum:
                        po.wait_ge(s, added(job - 1))
                    apart(po)
                count(po.tensor_copy(idx_cur[:, :], idx_next[:, :]),
                      po.tensor_copy(gate_cur[:, :], gate_next[:, :]))
                po.wait_ge(s_val, job + 1)
                v = lambda c: slot_val[:, :, c:c + 1].rearrange("p c o -> p (c o)")
                k = lambda c: kc[:, c:c + 2]
                count(po.tensor_tensor(tiny[:, 0], v(2), k(K_TAKE), ALU.mult),
                      po.tensor_tensor(tiny[:, 1], v(0), v(1), ALU.add),
                      po.tensor_tensor(tiny[:, 2], v(3), v(4), ALU.add))
                count(po.tensor_tensor(tiny[:, 0], k(K_OWN), tiny[:, 0], ALU.subtract),
                      po.tensor_tensor(tiny[:, 1], tiny[:, 1], k(K_SCALE), ALU.mult),
                      po.tensor_tensor(gate_next[:, :], tiny[:, 2], v(5), ALU.add))
                count(po.tensor_tensor(tiny[:, 1], tiny[:, 0], tiny[:, 1], ALU.add))
                count(po.tensor_copy(idx_next[:, :], tiny[:, 1]))
                assert n[0] == POOL_STEPS
                wait(po, s_xtr, job * 3)
                apart(po)
                for part, src, m, n in ((0, x1_rows, P, D), (1, x1_quarters, QP, QW)):
                    po.indirect_dma_start(out=x_rows[0:m, part, 0:n], out_offset=None, in_=src[:, :],
                                          in_offset=bass.IndirectOffsetOnAxis(ap=idx_next[0:m, part:part + 1], axis=0))\
                      .then_inc(s_gat[part], 16)

            def add_rows(j):
                po.wait_ge(s_yrow, rows_out(j))
                for part in range(2):
                    po.wait_ge(s_sum[part], j * 16 + 16)
                apart(po)
                for part, to, m, n in ((0, sum_rows, P, D), (1, sum_quarters, QP, QW)):
                    po.indirect_dma_start(out=to[:, :],
                                          out_offset=bass.IndirectOffsetOnAxis(ap=idx_cur[0:m, part:part + 1], axis=0),
                                          in_=y_rows[0:m, part, 0:n], in_offset=None, compute_op=ALU.add)\
                      .then_inc(s_sum[part], 16)

            po.tensor_copy(idx_next[:, :], kc[:, K_OWN:K_OWN + 2]).then_inc(s_init, 1)
            po.memset(gate_next[:, :], 0.0).then_inc(s_init, 1)
            po.wait_ge(s_init, 2)
            po.wait_ge(s_route, 1)
            columns(0, 0, 0)
            for s in s_st:
                po.wait_ge(s, NT // 2 * 32)
            for s in s_sum:
                po.wait_ge(s, 16)
            po.wait_ge(s_own, 32)
            rows(0)
            po.wait_ge(s_tab, 2)
            jobs = po.value_load(table[0:1, 0, TABLE - 1:TABLE], min_val=EXPERTS, max_val=JOBS)
            with po.Fori(0, jobs) as j:
                e = po.value_load(table[0:1, 0, bass.ds(j + 1, 1)], min_val=0, max_val=EXPERTS - 1)
                b = po.value_load(table[0:1, 1, bass.ds(j + 1, 1)], min_val=0, max_val=MORE + 1)
                columns(j + 1, e, b)
                def act_lo(u):
                    po.wait_ge(s_ahi, j * GU + u + 1)
                    po.tensor_tensor(act_parts[:, u, 1], act[:, u], act_parts[:, u, 0].bitcast(F32), ALU.subtract)\
                      .then_inc(s_alo, 1)

                for u in range(UNITS):
                    job, unit = of(j, u + LO_AHEAD)
                    if u == 4:
                        rows(j + 1)
                    if u == GU:
                        act_lo(u - 1)
                    if unit in POOL_LO:
                        lo_part(po, job, unit)
                    if 0 < u < GU:
                        act_lo(u - 1)
                    if u == 1:
                        add_rows(j)
            add_rows(jobs)
            po.wait_ge(s_gb2, 32)
            for i in range(NT):
                po.wait_ge(s_gx, NT + i + 1)
                po.tensor_tensor(fin[:, i], fin[:, i], gb2[:, 1], ALU.add).then_inc(s_x1, 1)


def constants():
    import numpy as np

    f = np.float32
    t = np.arange(P)
    row, col = t[:, None], t[None, :]
    parts = []
    for first in (False, True):
        for w in WINDOWS:
            n = np.minimum(col + 1, w) if first else np.full((1, P), w)
            parts.append(((row <= col) & (row > col - w)) / n - (row == col))
    parts.append(row < col)
    parts.append(np.tile((np.arange(NT * EXPERTS) % EXPERTS != 0)[None], (P, 1)))
    lists, e = np.divmod(np.arange(CANDIDATES), EXPERTS)
    loop = np.maximum(lists - MORE, 0)
    further = (lists > 0) & (lists <= MORE)
    level = np.where(further, SLOTS * lists, np.array(WIDTHS[1:] + (-1,))[loop])
    under = np.array((SEQ,) + WIDTHS[1:])[loop]
    level[(e == 0) & (lists == 0)] = -1
    level[(e == 0) & (lists > MORE)] = SEQ
    under[(e == 0) & (lists > MORE)] = SEQ
    part = np.where(lists <= MORE, lists, 0)
    parts += [np.tile(v[None], (P, 1)) for v in (level, under, e, part - (MORE + 1))]
    parts.append(row + 1)
    for i in range(NT):
        parts.append(np.concatenate([row, np.full((P, 1), i * P), np.ones((P, 1))], 1))
    consts = np.concatenate([p.astype(f) for p in parts], 1)
    assert consts.shape == (P, C_END)
    r, c = np.arange(HALO)[:, None], np.arange(HALO)[None, :]
    halo = np.concatenate([(r // REACH == c // REACH) * (r % REACH - REACH > c % REACH - w) / w for w in WINDOWS],
                          1).astype(f)
    own, own_tail = SEQ + row, SEQ + P + row % TAIL
    keep = np.concatenate([
        np.eye(P), np.tile(col, (P, 1)), np.tile(P + col[:, :QP] % TAIL, (P, 1)),
        own, QUARTERS * own_tail, np.full((P, 1), 1), np.full((P, 1), QUARTERS),
        own, QUARTERS * own_tail + row // TAIL,
        np.tile(SLOTS * np.arange(MORE + 2)[None], (P, 1))], 1).astype(f)
    assert keep.shape == (P, K_END)
    assert JOBS <= T_ENDS - 1 and (MORE + 1) * SLOTS >= SEQ
    return np.ascontiguousarray(consts), np.ascontiguousarray(keep), halo


def kernel(x, pool_w, pool_scale, sc_w_in, sc_conv_w, sc_w_out, cf_w_in, cf_b_in, cf_dw_w, cf_dw_b, cf_ln_g,
           cf_ln_b, cf_w_out, cf_b_out, mix_ln_g, mix_ln_b, router_w, router_b, moe_w_gu, moe_b_gu, moe_w_dn,
           moe_b_dn, ffn_ln_g, ffn_ln_b):
    import numpy as np
    import concourse.bacc as bacc
    from concourse.bass_utils import run_bass_kernel_spmd

    consts, keep, halo = constants()
    b_gu = np.asarray(moe_b_gu)[0].reshape(EXPERTS, KD, P, 2).transpose(0, 2, 3, 1).reshape(EXPERTS, P, 2 * KD)
    b_dn = np.asarray(moe_b_dn)[0].reshape(EXPERTS, KD, P).transpose(0, 2, 1)
    arrays = {
        "x": np.asarray(x)[0],
        "w_mix": np.asarray(pool_w)[0].reshape(D, 256),
        "mix_scale": np.asarray(pool_scale),
        "ln1": np.concatenate([np.asarray(mix_ln_g), np.asarray(mix_ln_b)]),
        "ln2": np.concatenate([np.asarray(ffn_ln_g), np.asarray(ffn_ln_b)]),
        "router_w": np.asarray(router_w)[0],
        "router_b": np.asarray(router_b),
        "w_gu": np.asarray(moe_w_gu)[0],
        "w_dn": np.asarray(moe_w_dn)[0],
        "biases": np.concatenate([b_gu, b_dn], 2),
        "keep": keep,
        "consts": consts,
        "halo": halo,
    }
    arrays = {n: np.ascontiguousarray(a) for n, a in arrays.items()}
    nc = bacc.Bacc("TRN2", target_bir_lowering=False, num_devices=1)
    args = [nc.dram_tensor(n, a.shape, mybir.dt.from_np(a.dtype), kind="ExternalInput").ap()
            for n, a in arrays.items()]
    out = nc.dram_tensor("out", (SEQ, D), F32, kind="ExternalOutput").ap()
    build_program(nc, *args, out)
    r = run_bass_kernel_spmd(nc, [arrays], core_ids=[0])
    return np.asarray(r.results[0]["out"]).reshape(1, SEQ, D)
```
